# Optimizing a Trainium2 kernel written in Bass

```python
import jax, jax.numpy as jnp
from jax import lax
import numpy as np

D_MODEL = 1024
BATCH = 1
SEQ = 256
DEPTH = 2

N_HEADS = 8
QK_NOPE_DIM = 128
QK_ROPE_DIM = 64
QK_DIM = QK_NOPE_DIM + QK_ROPE_DIM
V_HEAD_DIM = 128
Q_LORA_RANK = 384
KV_LORA_RANK = 256
ROPE_THETA = 10000.0
Q_BLOCK = 128
POOL_WINDOWS = (2, 4, 8, 16)
N_POOL_GROUPS = 4
POOL_GROUP_DIM = 128
POOL_DIM = N_POOL_GROUPS * POOL_GROUP_DIM
N_BRANCHES = 2
IN_DIM = POOL_DIM + Q_LORA_RANK + KV_LORA_RANK + QK_ROPE_DIM + N_BRANCHES * D_MODEL
SPLIT_POINTS = (POOL_DIM,
                POOL_DIM + Q_LORA_RANK,
                POOL_DIM + Q_LORA_RANK + KV_LORA_RANK,
                POOL_DIM + Q_LORA_RANK + KV_LORA_RANK + QK_ROPE_DIM)
D_FF = 2816
NORM_EPS = 1e-6

kernel_name = "macaron_gated_pool_mla_trunk"

def rms_norm(x, g):
    xf = x.astype(jnp.float32)
    y = xf * lax.rsqrt(jnp.mean(xf * xf, axis=-1, keepdims=True) + NORM_EPS)
    return (y * g.astype(jnp.float32)).astype(x.dtype)

def swiglu_ffn(h, w_up, w_down):
    gate, up = jnp.split(h @ w_up, 2, axis=-1)
    return (jax.nn.silu(gate) * up) @ w_down

def rope_tables(positions):
    inv_freq = ROPE_THETA ** (-jnp.arange(0, QK_ROPE_DIM, 2, dtype=jnp.float32) / QK_ROPE_DIM)
    ang = positions.astype(jnp.float32)[..., None] * inv_freq
    return jnp.cos(ang), jnp.sin(ang)

def apply_rope(x, cos, sin):
    xf = x.astype(jnp.float32)
    x1, x2 = jnp.split(xf, 2, axis=-1)
    out = jnp.concatenate([x1 * cos - x2 * sin, x2 * cos + x1 * sin], axis=-1)
    return out.astype(x.dtype)

def causal_multiscale_pool(xp, pool_maps, pool_scale):
    B, S, _ = xp.shape
    xg = xp.reshape(B, S, N_POOL_GROUPS, POOL_GROUP_DIM).astype(jnp.float32)
    csum = jnp.pad(jnp.cumsum(xg, axis=1), ((0, 0), (1, 0), (0, 0), (0, 0)))
    windows = jnp.array(POOL_WINDOWS, dtype=jnp.int32)
    t = jnp.arange(S, dtype=jnp.int32)[:, None]
    start = jnp.maximum(t + 1 - windows[None, :], 0)
    csum_start = csum[:, start, jnp.arange(N_POOL_GROUPS)[None, :]]
    count = jnp.minimum(t + 1, windows[None, :]).astype(jnp.float32)
    pooled = (csum[:, 1:] - csum_start) / count[None, :, :, None] - xg
    mixed = jnp.einsum('bsgc,gcd->bsgd', pooled.astype(xp.dtype), pool_maps)
    return mixed.reshape(B, S, POOL_DIM) * pool_scale

def mla_attention(q_lat, kv_lat, k_rope, cos, sin, q_norm, w_uq, kv_norm, w_ukv):
    B, S, _ = q_lat.shape
    q = (rms_norm(q_lat, q_norm) @ w_uq).reshape(B, S, N_HEADS, QK_DIM)
    q_nope, q_rope = q[..., :QK_NOPE_DIM], q[..., QK_NOPE_DIM:]
    kv = (rms_norm(kv_lat, kv_norm) @ w_ukv).reshape(B, S, N_HEADS, QK_NOPE_DIM + V_HEAD_DIM)
    k_nope, v = kv[..., :QK_NOPE_DIM], kv[..., QK_NOPE_DIM:]
    q_rope = apply_rope(q_rope, cos[:, :, None, :], sin[:, :, None, :])
    k_rope = apply_rope(k_rope, cos, sin)
    scale = QK_DIM ** -0.5
    outs = []
    for blk in range(S // Q_BLOCK):
        q0 = blk * Q_BLOCK
        k_end = q0 + Q_BLOCK
        s = (jnp.einsum('bqhd,bkhd->bhqk', q_nope[:, q0:k_end], k_nope[:, :k_end])
             + jnp.einsum('bqhr,bkr->bhqk', q_rope[:, q0:k_end], k_rope[:, :k_end]))
        s = s.astype(jnp.float32) * scale
        mask = (q0 + jnp.arange(Q_BLOCK))[:, None] >= jnp.arange(k_end)[None, :]
        s = jnp.where(mask[None, None], s, jnp.finfo(jnp.float32).min)
        p = jax.nn.softmax(s, axis=-1).astype(v.dtype)
        outs.append(jnp.einsum('bhqk,bkhd->bqhd', p, v[:, :k_end]))
    o = jnp.concatenate(outs, axis=1)
    return o.reshape(B, S, N_HEADS * V_HEAD_DIM)

def setup_inputs(seed: int = 0) -> dict:
    key = jax.random.key(seed)
    ks = jax.random.split(key, 24)
    f32 = jnp.float32

    def w(k, shape, fan_in):
        return jax.random.normal(k, shape, f32) * (fan_in ** -0.5)

    def gain(k, shape):
        return 1.0 + 0.02 * jax.random.normal(k, shape, f32)

    L, D = DEPTH, D_MODEL
    offsets = jax.random.randint(ks[1], (BATCH, 1), 0, 4096, dtype=jnp.int32)
    positions = offsets + jnp.arange(SEQ, dtype=jnp.int32)[None, :]
    return {
        "x": jax.random.normal(ks[0], (BATCH, SEQ, D), f32),
        "positions": positions,
        "norm_ffn1": gain(ks[2], (L, D)),
        "ffn1_up": w(ks[3], (L, D, 2 * D_FF), D),
        "ffn1_down": w(ks[4], (L, D_FF, D), D_FF),
        "norm_mix": gain(ks[5], (L, D)),
        "w_in": w(ks[6], (L, D, IN_DIM), D),
        "b_gate": 0.02 * jax.random.normal(ks[7], (L, N_BRANCHES * D), f32),
        "pool_maps": w(ks[8], (L, N_POOL_GROUPS, POOL_GROUP_DIM, POOL_GROUP_DIM), POOL_GROUP_DIM),
        "pool_scale": 1.0 + 0.1 * jax.random.normal(ks[9], (L, POOL_DIM), f32),
        "w_pool_proj": w(ks[10], (L, POOL_DIM, D), POOL_DIM),
        "q_latent_norm": gain(ks[11], (L, Q_LORA_RANK)),
        "w_uq": w(ks[12], (L, Q_LORA_RANK, N_HEADS * QK_DIM), Q_LORA_RANK),
        "kv_latent_norm": gain(ks[13], (L, KV_LORA_RANK)),
        "w_ukv": w(ks[14], (L, KV_LORA_RANK, N_HEADS * (QK_NOPE_DIM + V_HEAD_DIM)), KV_LORA_RANK),
        "w_attn_proj": w(ks[15], (L, N_HEADS * V_HEAD_DIM, D), N_HEADS * V_HEAD_DIM),
        "w_out": w(ks[16], (L, D, D), D),
        "norm_ffn2": gain(ks[17], (L, D)),
        "ffn2_up": w(ks[18], (L, D, 2 * D_FF), D),
        "ffn2_down": w(ks[19], (L, D_FF, D), D_FF),
        "final_norm": gain(ks[20], (D,)),
    }

def reference(x, positions, norm_ffn1, ffn1_up, ffn1_down, norm_mix, w_in, b_gate,
              pool_maps, pool_scale, w_pool_proj, q_latent_norm, w_uq, kv_latent_norm,
              w_ukv, w_attn_proj, w_out, norm_ffn2, ffn2_up, ffn2_down, final_norm):
    B, S, D = x.shape
    cos, sin = rope_tables(positions)
    for l in range(DEPTH):
        x = x + 0.5 * swiglu_ffn(rms_norm(x, norm_ffn1[l]), ffn1_up[l], ffn1_down[l])
        h = rms_norm(x, norm_mix[l])
        proj = h @ w_in[l]
        x_pool, q_lat, kv_lat, k_rope, gate_logits = jnp.split(proj, SPLIT_POINTS, axis=-1)
        gates = jax.nn.sigmoid((gate_logits + b_gate[l]).astype(jnp.float32)).astype(x.dtype)
        gates = gates.reshape(B, S, N_BRANCHES, D)
        branch_a = causal_multiscale_pool(x_pool, pool_maps[l], pool_scale[l]) @ w_pool_proj[l]
        branch_b = mla_attention(q_lat, kv_lat, k_rope, cos, sin, q_latent_norm[l], w_uq[l],
                                 kv_latent_norm[l], w_ukv[l]) @ w_attn_proj[l]
        merged = gates[:, :, 0] * branch_a + gates[:, :, 1] * branch_b
        x = x + merged @ w_out[l]
        x = x + 0.5 * swiglu_ffn(rms_norm(x, norm_ffn2[l]), ffn2_up[l], ffn2_down[l])
    return rms_norm(x, final_norm)


_drawn_inputs = setup_inputs


def setup_inputs(seed=0):
    import zlib

    import numpy as np

    out = dict(_drawn_inputs(seed))
    spreads = {}
    factors = {'norm_ffn1': 4.667,
     'norm_mix': 4.07,
     'b_gate': 8.0,
     'q_latent_norm': 8.0,
     'kv_latent_norm': 8.0,
     'norm_ffn2': 5.67,
     'final_norm': 2.956}
    for name, (base, spread) in spreads.items():
        noise = np.random.default_rng([zlib.crc32(name.encode()), seed]).standard_normal(out[name].shape)
        drawn = base * np.exp(spread * noise) if base else spread * noise
        out[name] = __import__('jax').numpy.asarray(drawn.astype(out[name].dtype))
    for name, factor in factors.items():
        out[name] = (out[name] * factor).astype(out[name].dtype)
    return out
```

```python
import numpy as np
from contextlib import ExitStack

import concourse.bass as bass
from concourse import mybir

F32 = mybir.dt.float32
F32R = mybir.dt.float32r
I32 = mybir.dt.int32
ACT = mybir.ActivationFunctionType
ALU = mybir.AluOpType
AX = mybir.AxisListType

P = 128
S, D, DEPTH = 256, 1024, 2
TB = S // P
KD = D // P
HEADS, NOPE, ROPE, VD = 8, 128, 64, 128
QK = NOPE + ROPE
QR, KVR = 384, 256
WINDOWS = (2, 4, 8, 16)
PG = len(WINDOWS)
POOL = PG * P
FF = 2816
EPS = 1e-6
THETA = 10000.0
SCALE = float(QK) ** -0.5
MASKED = -1e30

CH = 256
NCH = FF // CH
KCH = CH // P
GROUP = 2048
RING = 3
N512 = 512
PAIRS = HEADS // 2

C_POOL, C_Q, C_KV, C_GATE = 0, POOL, POOL + QR, POOL + QR + KVR + ROPE
KVW = KVR + ROPE

FFN_GROUPS = 3 * NCH
M_Q, M_KV, M_POOL, M_G0, M_G1, M_G2, M_MAPS, M_G3 = 0, 2, 4, 6, 8, 10, 12, 13
M_PAIR = 15
M_PP = M_PAIR + 2 * PAIRS
M_AP = M_PP + 2
M_WO = M_AP + 4
MIX_GROUPS = M_WO + 4
MIX0 = FFN_GROUPS
FFN2_0 = FFN_GROUPS + MIX_GROUPS
GROUPS = 2 * FFN_GROUPS + MIX_GROUPS
UPS = (NCH, 1, NCH - 1)
assert GROUPS % RING == 0 and FFN2_0 % RING == 0 and FFN_GROUPS % RING == 0

ROUND = 1.5 * 2.0 ** 23
TWO_PI = (6.28125, float(np.float32(0.0019350051879882812)), 3.0199159819344e-07)
PI_LOW = float(np.nextafter(np.float32(np.pi), np.float32(0)))

ROT_STEPS = 3 + TB + 2 * 5 + 4

GU_BANK, TR_BANK = 4, 6
NORM_T_BANK = (6, 0)
MERGE_T_BANK = (6, 4)


def shape_constants():
    ident = np.eye(P, dtype=np.float32)
    causal = np.zeros((P, S), np.float32)
    causal[:, P:] = np.where(np.arange(P)[:, None] >= np.arange(P)[None, :], 0.0, MASKED)
    t = np.arange(S)
    window = np.zeros((S, PG, S), np.float32)
    inv_count = np.zeros((PG, S), np.float32)
    for g, w in enumerate(WINDOWS):
        inside = (t[:, None] <= t[None, :]) & (t[:, None] > t[None, :] - w)
        count = np.minimum(t + 1, w)
        window[:, g] = inside - np.eye(S) * count[None, :]
        inv_count[g] = np.float32(1.0) / count.astype(np.float32)
    window = np.concatenate([window[:P].reshape(P, -1), window[P:, :, P:].reshape(P, -1)], axis=1)
    half = ROPE // 2
    freq = np.float32(THETA) ** (-np.arange(0, ROPE, 2, dtype=np.float32) / np.float32(ROPE))
    freq = freq.astype(np.float32)
    quarter = np.float32(np.pi / 2)
    freq_f = np.tile(freq, 4)[:, None] * np.ones((1, S), np.float32)
    phase_f = np.repeat([quarter, quarter, 0, 0], half)[:, None] * np.ones((1, S), np.float32)
    sign_f = np.repeat([1, 1, -1, 1], half)[:, None] * np.ones((1, S), np.float32)
    freq_t = np.tile(freq, 4 * TB)[None] * np.ones((P, 1), np.float32)
    phase_t = np.tile(np.repeat([quarter, quarter, 0, 0], half), TB)[None] * np.ones((P, 1), np.float32)
    sign_t = np.tile(np.repeat([1, 1, -1, 1], half), TB)[None] * np.ones((P, 1), np.float32)
    rotary = np.stack([np.concatenate([a, b], axis=1) for a, b in
                       ((freq_f, freq_t), (phase_f, phase_t), (sign_f, sign_t))], axis=1)
    return {
        "c_ident": ident, "c_causal": causal, "c_window": window.astype(np.float32),
        "c_inv_count": inv_count.reshape(1, -1), "c_rotary": rotary.astype(np.float32),
    }


class Event:

    def __init__(self, sem, per_layer, first=0):
        self.sem, self.per_layer, self.first = sem, per_layer, first

    def upto(self, layer, n):
        return layer * self.per_layer + (n + self.first)


def trunk(nc, x_in, positions, gains, ffn1_up, ffn1_down, w_in, b_gate, pool_maps, pool_scale,
          w_pool_proj, q_latent_norm, w_uq, kv_latent_norm, w_ukv, w_attn_proj, w_out,
          ffn2_up, ffn2_down, c_ident, c_causal, c_window, c_inv_count, c_rotary, out):
    with ExitStack() as ctx:
        def sb(name, shape, dt=F32):
            return ctx.enter_context(nc.sbuf_tensor(name, shape, dt))

        def sem(name):
            return ctx.enter_context(nc.semaphore(name))

        def event(name, per_layer, first=0):
            return Event(sem(name), per_layer, first)

        x = sb("x", [P, TB, D])
        xs = sb("xs", [P, TB, D])
        raw = sb("raw", [P, RING, GROUP])
        w_hi = sb("w_hi", [P, RING, GROUP], F32R)
        w_lo = sb("w_lo", [P, RING, GROUP], F32R)
        xT = sb("xT", [P, 2, KD, S], F32R)
        pair1 = sb("pair1", [P, 2, KD, S], F32R)
        small_T = sb("small_T", [P, 2, 4 * S], F32R)
        latT = sb("latT", [P, 2, 3 + 3, S], F32R)
        oT = sb("oT", [P, 2, HEADS, S], F32R)
        xp = sb("xp", [P, 2, PG * S], F32R)
        window = sb("window", [P, PG * (S + P)], F32R)
        gates = sb("gates", [P, TB, 2 * D])
        scores = sb("scores", [P, 2, 3 * S])
        ident = sb("ident", [P, P])
        causal = sb("causal", [P, S])
        inv_count = sb("inv_count", [P, PG * S])
        gain = sb("gain", [P, D])
        lat_gain = sb("lat_gain", [P, QR + KVR])
        rot = sb("rot", [P, 2 * S])
        pscale = sb("pscale", [P, DEPTH, PG])
        stat = sb("stat", [P, 32])
        psum = ctx.enter_context(nc.psum_tensor("psum", [P, 8, N512], F32))

        silu_sb = scores[:, 0, 0:TB * CH].rearrange("p (t n) -> p t n", t=TB)
        act_sb = scores[:, 1, 0:TB * CH].rearrange("p (t n) -> p t n", t=TB)
        tmp = scores[:, :, :].rearrange("p a n -> p (a n)")[:, 0:PG * S]
        poolT = oT[:, :, 0:PG, :]
        mixT = xp[:, :, :].rearrange("p s (g t) -> p s g t", g=PG)
        xpt = xp[:, :, :].rearrange("p s (t n) -> p s t n", t=TB)
        qlat_s = xs[:, 0, 0:TB * QR].rearrange("p (t n) -> p t n", t=TB)
        kvlat_s = xs[:, 1, 0:TB * 3 * P].rearrange("p (t n) -> p t n", t=TB)
        rot_a = xs[:, 1, 3 * S:3 * S + TB * ROPE].rearrange("p (t n) -> p t n", t=TB)
        rot_b = xs[:, 1, 3 * S + TB * ROPE:3 * S + 2 * TB * ROPE].rearrange("p (t n) -> p t n", t=TB)
        qlT, kvT, krT = latT[:, :, 0:3, :], latT[:, :, 3:5, :], latT[:, :, 5, :]
        rot_f = rot[:, 0:S]
        rot_t = rot[:, S:2 * S].rearrange("p (t c n) -> p t c n", t=TB, c=2)
        QN, QRO, KN, VV = range(4)

        def pair(p, part):
            buf = (xT, pair1)[p % 2]
            return buf[:, :, 2 * part:2 * part + 2, :]

        NSQ, NMS, NRS = 0, 2, 4
        LSQ, LMS, LRS = 6, 10, 14
        SMX, SNM, SSUM, SINV = 18, 22, 26, 28
        stat2 = sb("stat2", [P, 2, 16])
        half_neg = sb("half_neg", [P, 4])
        pos_col_i, pos_col = sb("pos_col_i", [P, TB], I32), sb("pos_col", [P, TB])
        pos_row_i = gates[:, 0, 0:S].bitcast(I32)
        pos_row = gates[:, 0, S:2 * S]
        turns = gates[:, 0, 2 * S:4 * S]
        angle = gates[:, 0, 4 * S:6 * S]
        rotary = gates[:, 1, 0:6 * S].rearrange("p (c n) -> p c n", c=3)
        freq, phase, sign = (rotary[:, i, :] for i in range(3))
        window_f = scores[:, :, :].rearrange("p a n -> p (a n)")
        ROWS = (slice(0, S), slice(S, 2 * S), slice(2 * S, 2 * S + P), slice(2 * S + P, 3 * S))

        loads_begun = sem("loads_begun")
        raw_landed = [sem(f"raw_landed{i}") for i in range(RING)]
        x_landed, const_landed, out_landed = sem("x_landed"), sem("const_landed"), sem("out_landed")
        gain_landed, latg_landed, bias_landed = sem("gain_landed"), sem("latg_landed"), sem("bias_landed")
        w_hi_done = event("w_hi_done", GROUPS)
        w_lo_done = event("w_lo_done", GROUPS, RING)
        w_used = event("w_used", GROUPS, RING)
        exponent_set, pos_landed = sem("exponent_set"), sem("pos_landed")
        rot_step, rot_sin, setup_done = sem("rot_step"), sem("rot_sin"), sem("setup_done")
        x_ready = event("x_ready", 3 * TB, TB)
        sq_done = event("sq_done", 3 * TB)
        ms_done = event("ms_done", 3 * TB)
        rstd_done = event("rstd_done", 3 * TB)
        normed = event("normed", 3 * TB)
        norm_tr = event("norm_tr", 3 * TB)
        norm_hi = event("norm_hi", 3 * TB)
        norm_lo = event("norm_lo", 3 * TB)
        gu_done = event("gu_done", 2 * NCH)
        silu_done = event("silu_done", 2 * NCH * TB)
        act_done = event("act_done", 2 * NCH * TB)
        hid_tr = event("hid_tr", 2 * NCH)
        hid_hi = event("hid_hi", 2 * NCH)
        hid_lo = event("hid_lo", 2 * NCH)
        y_done = event("y_done", 3)
        q_done, kv_done, xp_done = event("q_done", 1), event("kv_done", 1), event("xp_done", 1)
        lat_sq = event("lat_sq", 2 * TB)
        lat_ms = event("lat_ms", 2)
        lat_rstd = event("lat_rstd", 2)
        lat_normed = event("lat_normed", 2)
        krot_step = event("krot_step", 3)
        lat_tr, lat_hi, lat_lo = event("lat_tr", 2 * TB), event("lat_hi", 2 * TB), event("lat_lo", 2 * TB)
        xp_hi, xp_lo = event("xp_hi", TB), event("xp_lo", TB)
        gate_done, gate_biased, gate_sig = event("gate_done", 4), event("gate_biased", 4 * TB), event("gate_sig", 4 * TB)
        pool_done, pool_scaled = event("pool_done", 1), event("pool_scaled", 2)
        pool_hi, pool_lo = event("pool_hi", 2), event("pool_lo", 2)
        part_done = event("part_done", 2 * PAIRS)
        rope_done = event("rope_done", PAIRS)
        part_hi, part_lo = event("part_hi", 4 * PAIRS), event("part_lo", 4 * PAIRS)
        score_done, score_masked = event("score_done", PAIRS), event("score_masked", PAIRS)
        max_done, bias_done, exp_done = event("max_done", PAIRS), event("bias_done", PAIRS), event("exp_done", PAIRS)
        inv_done, prob_done = event("inv_done", PAIRS), event("prob_done", PAIRS)
        prob_tr, prob_hi, prob_lo = event("prob_tr", PAIRS), event("prob_hi", PAIRS), event("prob_lo", PAIRS)
        pv_done, o_hi, o_lo = event("pv_done", PAIRS), event("o_hi", PAIRS), event("o_lo", PAIRS)
        a_done, a_gated = event("a_done", 2), event("a_gated", 2 * TB)
        b_done, b_gated, merged = event("b_done", 2), event("b_gated", 2 * TB), event("merged", 2 * TB)
        mrg_tr, mrg_hi, mrg_lo = event("mrg_tr", TB), event("mrg_hi", TB), event("mrg_lo", TB)

        ups, downs = (ffn1_up, ffn2_up), (ffn1_down, ffn2_down)

        def blk(t):
            return slice(t * P, (t + 1) * P)

        def flat(v, i):
            return v[:, i].rearrange("p a n -> p (a n)")

        def products(eng, L, ev, i, t, g):
            if t == 0:
                eng.wait_ge(ev.sem, ev.upto(L, i + 1))
            else:
                eng.wait_ge(w_used.sem, w_used.upto(L, g + 1))

        def hid_cols(j):
            return slice(KCH * S, 2 * KCH * S) if isinstance(j, int) and j == NCH - 1 else slice(0, KCH * S)

        def gu_group(f, j):
            return f * FFN2_0 + (1 if isinstance(j, int) and j == 0 else 3 * j)

        def part_products(eng, L, p, part):
            products(eng, L, part_done, 2 * p + part // 2, part % 2, MIX0 + M_PAIR + 2 * p + part // 2)

        def banks(b):
            return psum[:, b:b + 2, :].rearrange("p b n -> p (b n)")

        def mix_source(m, L):
            def rows(w, a, k, c0, n):
                return w[L, a * P:(a + k) * P, c0:c0 + n].rearrange("(k p) n -> p k n", p=P)
            if m < M_KV:
                return rows(w_in, 4 * (m - M_Q), 4, C_Q, QR)
            if m < M_POOL:
                return rows(w_in, 4 * (m - M_KV), 4, C_KV, KVW)
            if m < M_G0:
                return rows(w_in, 4 * (m - M_POOL), 4, C_POOL, POOL)
            for c, m0 in enumerate((M_G0, M_G1, M_G2, M_G3)):
                if m0 <= m < m0 + 2:
                    return rows(w_in, 4 * (m - m0), 4, C_GATE + c * N512, N512)
            if m == M_MAPS:
                return pool_maps[L].rearrange("g c d -> c g d")
            if m < M_PP:
                p, kv = (m - M_PAIR) // 2, (m - M_PAIR) % 2
                return rows(w_ukv, 0, 2, p * N512, N512) if kv else rows(w_uq, 0, 3, p * 2 * QK, 2 * QK)
            if m < M_AP:
                return rows(w_pool_proj, 0, 4, (m - M_PP) * N512, N512)
            w, i = (w_attn_proj, m - M_AP) if m < M_WO else (w_out, m - M_WO)
            return rows(w, 4 * (i % 2), 4, (i // 2) * N512, N512)

        def split_pieces(m):
            if m is None or m < M_PAIR or m >= M_PP or (m - M_PAIR) % 2:
                n = GROUP
                if m is not None:
                    k, w = {M_Q: (4, QR), M_KV: (4, KVW), M_MAPS: (PG, P)}.get(m if m != 1 and m != 3 else m - 1, (4, N512))
                    if M_PAIR <= m < M_PP:
                        k = 2
                    n = k * w
                return [(lambda s: s[:, 0:n], lambda s: s[:, 0:n])]
            def dst(a, b):
                return lambda s: s[:, 0:3 * N512].rearrange("p (k h n) -> p k h n", k=3, n=P)[:, :, 2:4, a:b]
            def src(a, b):
                return lambda s: s[:, 0:6 * QK].rearrange("p (k h n) -> p k h n", k=3, h=2)[:, :, :, a:b]
            h = ROPE // 2
            return [(lambda s: s[:, 0:3 * N512].rearrange("p (k h n) -> p k h n", k=3, n=P)[:, :, 0:2, :], src(0, NOPE)),
                    (dst(0, 2 * h), src(NOPE, QK)),
                    (dst(2 * h, 3 * h), src(NOPE + h, QK)),
                    (dst(3 * h, 4 * h), src(NOPE, NOPE + h))]

        block = ctx.enter_context(nc.Block())

        @block.sync
        def _(sp):
            sp.dma_start(x[:, :, :], x_in.rearrange("b (t p) d -> p (b t) d", p=P)).then_inc(x_landed, 16)

            def load(L, q, r, src, dst=None):
                if dst is None:
                    k, n = src.shape[1:]
                    dst = raw[:, r, 0:k * n].rearrange("p (k n) -> p k n", k=k)
                sp.wait_ge(w_lo_done.sem, w_lo_done.upto(L, RING * q + r + 1 - RING))
                sp.sem_inc(loads_begun, 1)
                sp.dma_start(dst, src).then_inc(raw_landed[r], 16)

            def load_up(L, f, q, r, j, a):
                src = ups[f][L, a * 4 * P:(a + 1) * 4 * P, :].rearrange("(k p) (u n) -> p k u n", p=P, u=2)
                dst = raw[:, r, :].rearrange("p (k u n) -> p k u n", k=4, u=2)
                load(L, q, r, src[:, :, 0, bass.ds(j * CH, CH)], dst[:, :, 0, :])
                sp.dma_start(dst[:, :, 1, :], src[:, :, 1, bass.ds(j * CH, CH)]).then_inc(raw_landed[r], 16)

            def load_down(L, f, q, r, j):
                load(L, q, r, downs[f][L, bass.ds(j * CH, CH), :].rearrange("(k p) n -> p k n", p=P))

            def ffn(L, f):
                q0 = f * FFN2_0 // RING
                load_up(L, f, q0, 0, 0, 0)
                load_up(L, f, q0, 1, 0, 1)
                with nc.sync.Fori(1, NCH) as j:
                    load_up(L, f, q0 + j - 1, 2, j, 0)
                    load_up(L, f, q0 + j, 0, j, 1)
                    load_down(L, f, q0 + j, 1, j - 1)
                load_down(L, f, q0 + NCH - 1, 2, NCH - 1)

            with nc.sync.Fori(0, DEPTH) as L:
                ffn(L, 0)
                for m in range(MIX_GROUPS):
                    load(L, (MIX0 + m) // RING, m % RING, mix_source(m, L))
                ffn(L, 1)

            out_v = out.rearrange("b (t p) d -> p (b t) d", p=P)
            for t in range(TB):
                sp.wait_ge(normed.sem, normed.upto(DEPTH, t + 1))
                sp.dma_start(out_v[:, t], xs[:, t, :]).then_inc(out_landed, 16)
            sp.wait_ge(out_landed, 16 * TB)

        @block.gpsimd
        def _(pool):
            def broadcast(dst, src, landed):
                return pool.dma_start(dst, src.to_broadcast(list(dst.shape))).then_inc(landed, 16)

            pool.memset(half_neg[:, :], -0.5).then_inc(exponent_set, 1)
            pool.dma_start(pos_row_i, positions[0:1, :].to_broadcast([P, S])).then_inc(pos_landed, 16)
            with nc.allow_non_contiguous_dma(reason="256 positions"):
                pool.dma_start(pos_col_i[:, :], positions.rearrange("b (t p) -> p (b t)", p=P)).then_inc(pos_landed, 16)
            pool.dma_start(rotary, c_rotary).then_inc(pos_landed, 16)
            pool.dma_start(ident[:, :], c_ident).then_inc(const_landed, 16)
            broadcast(gain[:, :], gains[0:1, :], gain_landed)
            pool.dma_start(causal[:, :], c_causal).then_inc(const_landed, 16)
            pool.dma_start(window_f, c_window).then_inc(const_landed, 16)
            broadcast(inv_count[:, :], c_inv_count, const_landed)
            with nc.allow_non_contiguous_dma(reason="1024 scales"):
                pool.dma_start(pscale[:, :, :], pool_scale.rearrange("l (g p) -> p l g", p=P)).then_inc(const_landed, 16)

            def rsqrt(dst, src, width, done):
                pool.tensor_tensor(dst, src, half_neg[:, 0:width], ALU.pow).then_inc(done.sem, 1)

            pool.wait_ge(exponent_set, 1)
            with nc.gpsimd.Fori(0, DEPTH) as L:
                for s in range(3):
                    for t in range(TB):
                        pool.wait_ge(ms_done.sem, ms_done.upto(L, TB * s + t + 1))
                        rsqrt(stat[:, NRS + t:NRS + t + 1], stat[:, NMS + t:NMS + t + 1], 1, rstd_done)
                    if s == 0:
                        broadcast(lat_gain[:, 0:QR], q_latent_norm[bass.ds(L, 1), :], latg_landed)
                        broadcast(lat_gain[:, QR:QR + KVR], kv_latent_norm[bass.ds(L, 1), :], latg_landed)
                        for t in range(TB):
                            broadcast(gates[:, t, :], b_gate[bass.ds(L, 1), :], bias_landed)
                    pool.wait_ge(normed.sem, normed.upto(L, TB * s + TB))
                    broadcast(gain[:, :], gains[bass.ds(L * 3 + s + 1, 1), :], gain_landed)
                    if s == 1:
                        for i in range(2):
                            pool.wait_ge(lat_ms.sem, lat_ms.upto(L, i + 1))
                            rsqrt(stat[:, LRS + 2 * i:LRS + 2 * i + 2], stat[:, LMS + 2 * i:LMS + 2 * i + 2], 2, lat_rstd)
            for t in range(TB):
                pool.wait_ge(ms_done.sem, ms_done.upto(DEPTH, t + 1))
                rsqrt(stat[:, NRS + t:NRS + t + 1], stat[:, NMS + t:NMS + t + 1], 1, rstd_done)

        @block.scalar
        def _(act):
            def split(L, q, r, m=None, twos=0):
                per_layer = GROUPS // RING + 2 * UPS[r]
                act.wait_ge(raw_landed[r], (L * per_layer + q + 1 + twos) * 16)
                act.wait_ge(w_used.sem, w_used.upto(L, RING * q + r + 1 - RING))
                for dst, src in split_pieces(m):
                    last = act.activation(dst(w_hi[:, r, :]), src(raw[:, r, :]), ACT.Copy)
                last.then_inc(w_hi_done.sem, 1)

            def split_mix(L, m):
                if m < MIX_GROUPS:
                    split(L, (MIX0 + m) // RING, m % RING, m, UPS[m % RING])
                else:
                    r = m - MIX_GROUPS
                    split(L, FFN2_0 // RING, r, None, UPS[r] + 1)

            def high(L, after, n, dst, src, done):
                act.wait_ge(after.sem, after.upto(L, n))
                act.activation(dst, src, ACT.Copy).then_inc(done.sem, 1)

            def squares(L, s):
                for t in range(TB):
                    act.wait_ge(x_ready.sem, x_ready.upto(L, TB * s + t + 1 - TB))
                    act.activation(xs[:, t, :], x[:, t, :], ACT.Square,
                                   accum_out=stat[:, NSQ + t:NSQ + t + 1]).then_inc(sq_done.sem, 1)

            def norm(L, s):
                for t in range(TB):
                    high(L, norm_tr, TB * s + t + 1, xT[:, 0, :, blk(t)],
                         banks(NORM_T_BANK[t]).rearrange("p (k n) -> p k n", k=KD), norm_hi)

            def silu(L, f, j):
                for t in range(TB):
                    products(act, L, gu_done, f * NCH + j, t, gu_group(f, j))
                    act.activation(silu_sb[:, t, :], psum[:, GU_BANK + t, 0:CH], ACT.Silu).then_inc(silu_done.sem, 1)

            def hidden(L, f, j):
                high(L, hid_tr, f * NCH + j + 1, small_T[:, 0, hid_cols(j)], psum[:, TR_BANK, :], hid_hi)

            def ffn(L, f):
                q0 = f * FFN2_0 // RING
                u0, u2 = f * UPS[0], f * UPS[2]
                split(L, q0, 2, None, u2 + 1)
                silu(L, f, 0)
                split(L, q0 + 1, 0, None, u0 + 2)
                with nc.scalar.Fori(1, NCH - 1) as j:
                    split(L, q0 + j, 1, None, (f + 1) * UPS[1])
                    hidden(L, f, j - 1)
                    split(L, q0 + j, 2, None, u2 + j + 1)
                    silu(L, f, j)
                    split(L, q0 + j + 1, 0, None, u0 + j + 2)
                j = NCH - 1
                split(L, q0 + j, 1, None, (f + 1) * UPS[1])
                hidden(L, f, j - 1)
                split(L, q0 + j, 2, None, u2 + UPS[2])
                silu(L, f, j)
                if f == 0:
                    split_mix(L, 0)
                hidden(L, f, j)

            def parts(L, p, which):
                for part in which:
                    src = psum[:, 2 + part, :]
                    if part == QRO:
                        high(L, rope_done, p + 1, flat(pair(p, part), 0), src, part_hi)
                        continue
                    if part == VV and p >= 2:
                        act.wait_ge(pv_done.sem, pv_done.upto(L, p - 1))
                    part_products(act, L, p, part)
                    act.activation(flat(pair(p, part), 0), src, ACT.Copy).then_inc(part_hi.sem, 1)

            def softmax(L, p):
                row = scores[:, p % 2, :]
                st = stat2[:, p % 2, :]
                act.wait_ge(bias_done.sem, bias_done.upto(L, p + 1))
                for i, cols in enumerate(ROWS):
                    last = act.activation(row[:, cols], row[:, cols], ACT.Exp, scale=SCALE,
                                          bias=st[:, 4 + i:5 + i], accum_out=st[:, 8 + i:9 + i])
                last.then_inc(exp_done.sem, 1)

            def probs(L, p):
                high(L, prob_tr, p + 1, small_T[:, 0, 0:3 * S], banks(0)[:, 0:3 * S], prob_hi)

            def heads_out(L, p):
                high(L, pv_done, p + 1, flat(oT[:, :, 2 * p:2 * p + 2, :], 0), psum[:, 0, :], o_hi)

            def gate(L, c):
                for t in range(TB):
                    g = gates[:, t, c * N512:(c + 1) * N512]
                    act.wait_ge(gate_biased.sem, gate_biased.upto(L, TB * c + t + 1))
                    act.activation(g, g, ACT.Sigmoid).then_inc(gate_sig.sem, 1)

            def latent_squares(L, i):
                done, m, bank, dst, n = ((q_done, M_Q, 4, qlat_s, QR), (kv_done, M_KV, 2, kvlat_s, KVR))[i]
                for t in range(TB):
                    products(act, L, done, 0, t, MIX0 + m + 1)
                    c = LSQ + 2 * i + t
                    act.activation(dst[:, t, 0:n], psum[:, bank + t, 0:n], ACT.Square,
                                   accum_out=stat[:, c:c + 1]).then_inc(lat_sq.sem, 1)

            def latent(L, i):
                for t in range(TB):
                    high(L, lat_tr, 2 * i + t + 1, latT[:, 0, 3 * i:3 * i + 3, blk(t)],
                         psum[:, (4, 2)[i] + t, 0:3 * P].rearrange("p (k n) -> p k n", k=3), lat_hi)

            def mixer(L):
                split_mix(L, 2)
                split_mix(L, 3)
                latent_squares(L, 0)
                split_mix(L, 4)
                split_mix(L, 5)
                latent_squares(L, 1)
                split_mix(L, 6)
                split_mix(L, 7)
                for t in range(TB):
                    products(act, L, xp_done, 0, t, MIX0 + M_POOL + 1)
                    act.activation(xpt[:, 0, t, :], psum[:, 6 + t, :], ACT.Copy).then_inc(xp_hi.sem, 1)
                split_mix(L, 8)
                split_mix(L, 9)
                gate(L, 0)
                latent(L, 0)
                split_mix(L, 10)
                split_mix(L, 11)
                gate(L, 1)
                latent(L, 1)
                high(L, pool_scaled, 1, flat(poolT, 0), tmp, pool_hi)
                split_mix(L, 12)
                split_mix(L, 13)
                gate(L, 2)
                split_mix(L, 14)
                high(L, pool_scaled, 2, flat(mixT, 0), tmp, pool_hi)
                split_mix(L, 15)
                split_mix(L, 16)
                gate(L, 3)
                split_mix(L, 17)
                parts(L, 0, (QN, QRO))
                split_mix(L, 18)
                parts(L, 0, (KN, VV))
                split_mix(L, 19)
                parts(L, 1, (QN, QRO))
                split_mix(L, 20)
                parts(L, 1, (KN, VV))
                softmax(L, 0)
                split_mix(L, 21)
                parts(L, 2, (QN, QRO))
                split_mix(L, 22)
                parts(L, 2, (KN,))
                probs(L, 0)
                softmax(L, 1)
                heads_out(L, 0)
                parts(L, 2, (VV,))
                split_mix(L, 23)
                parts(L, 3, (QN, QRO))
                split_mix(L, 24)
                parts(L, 3, (KN,))
                probs(L, 1)
                softmax(L, 2)
                heads_out(L, 1)
                parts(L, 3, (VV,))
                split_mix(L, 25)
                probs(L, 2)
                softmax(L, 3)
                heads_out(L, 2)
                split_mix(L, 26)
                probs(L, 3)
                split_mix(L, 27)
                heads_out(L, 3)
                split_mix(L, 28)
                split_mix(L, 29)
                split_mix(L, 30)
                for t in range(TB):
                    high(L, mrg_tr, t + 1, xT[:, 0, :, blk(t)],
                         banks(MERGE_T_BANK[t]).rearrange("p (k n) -> p k n", k=KD), mrg_hi)
                for m in range(31, 35):
                    split_mix(L, m)

            act.wait_ge(rot_step, ROT_STEPS)
            act.activation(rot[:, :], angle, ACT.Sin).then_inc(rot_sin, 1)
            act.wait_ge(const_landed, 16 * 5)
            act.activation(window[:, :], window_f, ACT.Copy).then_inc(setup_done, 1)
            act.wait_ge(exponent_set, 1)
            act.activation(half_neg[:, 3:4], half_neg[:, 2:3], ACT.Silu)
            with nc.scalar.Fori(0, DEPTH) as L:
                split(L, 0, 0, None, 1)
                split(L, 0, 1, None, 1)
                squares(L, 0)
                norm(L, 0)
                ffn(L, 0)
                squares(L, 1)
                split_mix(L, 1)
                norm(L, 1)
                mixer(L)
                squares(L, 2)
                norm(L, 2)
                ffn(L, 1)
            squares(DEPTH, 0)

        @block.vector
        def _(dve):
            step = [0]

            def rot_op(ins):
                step[0] += 1
                ins.then_inc(rot_step, 1)
                dve.wait_ge(rot_step, step[0])

            def mul_add(dst, a, c, b):
                return dve.scalar_tensor_tensor(out=dst, in0=a, scalar=c, in1=b, op0=ALU.mult, op1=ALU.add)

            def times(dst, a, b):
                return dve.tensor_tensor(dst, a, b, ALU.mult)

            def rotary_setup():
                dve.wait_ge(pos_landed, 16 * 3)
                rot_op(dve.tensor_copy(pos_row, pos_row_i))
                rot_op(dve.tensor_copy(pos_col[:, :], pos_col_i[:, :]))
                rot_op(times(angle[:, 0:S], pos_row, freq[:, 0:S]))
                for t in range(TB):
                    cols = slice(S + t * P, S + (t + 1) * P)
                    rot_op(dve.tensor_scalar(angle[:, cols], freq[:, cols], pos_col[:, t:t + 1], None, ALU.mult))
                for unit in (1024.0, 1.0):
                    rot_op(dve.tensor_scalar(turns, angle, 1.0 / (2 * np.pi * unit), ROUND, ALU.mult, ALU.add))
                    rot_op(dve.tensor_scalar(turns, turns, -ROUND, None, ALU.add))
                    for c in TWO_PI:
                        rot_op(mul_add(angle, turns, -c * unit, angle))
                rot_op(dve.tensor_tensor(angle, angle, phase, ALU.add))
                rot_op(dve.tensor_scalar(turns, angle, PI_LOW, -2 * np.pi, ALU.is_gt, ALU.mult))
                rot_op(dve.tensor_tensor(angle, angle, turns, ALU.add))
                rot_op(dve.tensor_scalar(angle, angle, PI_LOW, -PI_LOW, ALU.min, ALU.max))
                assert step[0] == ROT_STEPS
                dve.wait_ge(rot_sin, 1)
                times(rot[:, :], rot[:, :], sign).then_inc(setup_done, 1)
                dve.wait_ge(setup_done, 2)

            def minus(dst, a, b):
                return dve.tensor_tensor(dst, a, b, ALU.subtract)

            def split(L, q, r, m=None):
                dve.wait_ge(w_hi_done.sem, w_hi_done.upto(L, RING * q + r + 1))
                for dst, src in split_pieces(m):
                    last = minus(dst(w_lo[:, r, :]), src(raw[:, r, :]), dst(w_hi[:, r, :].bitcast(F32)))
                last.then_inc(w_lo_done.sem, 1)

            def split_mix(L, m):
                if m < MIX_GROUPS:
                    split(L, (MIX0 + m) // RING, m % RING, m)
                else:
                    split(L, FFN2_0 // RING, m - MIX_GROUPS)

            def low(L, high_done, n, dst, src, hi, done):
                dve.wait_ge(high_done.sem, high_done.upto(L, n))
                minus(dst, src, hi.bitcast(F32)).then_inc(done.sem, 1)

            def add_half(L, s):
                for t in range(TB):
                    products(dve, L, y_done, s, t, FFN_GROUPS - 1 if s == 0 else GROUPS - 1)
                    mul_add(x[:, t, :], banks(2 * t), 0.5, x[:, t, :]).then_inc(x_ready.sem, 1)

            def mean_squares(L, s, t):
                dve.wait_ge(sq_done.sem, sq_done.upto(L, TB * s + t + 1))
                dve.tensor_scalar(stat[:, NMS + t:NMS + t + 1], stat[:, NSQ + t:NSQ + t + 1], 1.0 / D, EPS,
                                  ALU.mult, ALU.add).then_inc(ms_done.sem, 1)

            def scale_rows(L, s, t):
                dve.wait_ge(rstd_done.sem, rstd_done.upto(L, TB * s + t + 1))
                dve.wait_ge(gain_landed, (L * 3 + s + 1) * 16)
                dve.scalar_tensor_tensor(out=xs[:, t, :], in0=x[:, t, :], scalar=stat[:, NRS + t:NRS + t + 1],
                                         in1=gain[:, :], op0=ALU.mult, op1=ALU.mult).then_inc(normed.sem, 1)

            def norm(L, s, prepare):
                mean_squares(L, s, 0)
                mean_squares(L, s, 1)
                scale_rows(L, s, 0)
                scale_rows(L, s, 1)
                prepare()
                for t in range(TB):
                    low(L, norm_hi, TB * s + t + 1, xT[:, 1, :, blk(t)],
                        banks(NORM_T_BANK[t]).rearrange("p (k n) -> p k n", k=KD), xT[:, 0, :, blk(t)], norm_lo)

            def hidden_product(L, f, j):
                for t in range(TB):
                    n = (f * NCH + j) * TB + t + 1
                    dve.wait_ge(silu_done.sem, silu_done.upto(L, n))
                    times(act_sb[:, t, :], silu_sb[:, t, :], psum[:, GU_BANK + t, CH:2 * CH]).then_inc(act_done.sem, 1)

            def hidden(L, f, j):
                low(L, hid_hi, f * NCH + j + 1, small_T[:, 1, hid_cols(j)], psum[:, TR_BANK, :],
                    small_T[:, 0, hid_cols(j)], hid_lo)

            def ffn(L, f):
                q0 = f * FFN2_0 // RING
                split(L, q0, 2)
                hidden_product(L, f, 0)
                split(L, q0 + 1, 0)
                with nc.vector.Fori(1, NCH - 1) as j:
                    split(L, q0 + j, 1)
                    hidden(L, f, j - 1)
                    split(L, q0 + j, 2)
                    hidden_product(L, f, j)
                    split(L, q0 + j + 1, 0)
                j = NCH - 1
                split(L, q0 + j, 1)
                hidden(L, f, j - 1)
                split(L, q0 + j, 2)
                hidden_product(L, f, j)
                if f == 0:
                    split_mix(L, 0)
                hidden(L, f, j)
                add_half(L, 2 * f)

            def gate(L, c):
                for t in range(TB):
                    g = gates[:, t, c * N512:(c + 1) * N512]
                    dve.wait_ge(bias_landed, (L + 1) * 16 * TB)
                    products(dve, L, gate_done, c, t, MIX0 + (M_G0, M_G1, M_G2, M_G3)[c] + 1)
                    dve.tensor_tensor(g, psum[:, t, :], g, ALU.add).then_inc(gate_biased.sem, 1)

            def latent_norm(L, i):
                bank, dst, n, g0 = ((4, qlat_s, QR, 0), (2, kvlat_s, KVR, QR))[i]
                dve.wait_ge(lat_rstd.sem, lat_rstd.upto(L, i + 1))
                dve.wait_ge(latg_landed, (L + 1) * 32)
                for t in range(TB):
                    c = LRS + 2 * i + t
                    last = dve.scalar_tensor_tensor(out=dst[:, t, 0:n], in0=psum[:, bank + t, 0:n],
                                                    scalar=stat[:, c:c + 1], in1=lat_gain[:, g0:g0 + n],
                                                    op0=ALU.mult, op1=ALU.mult)
                last.then_inc(lat_normed.sem, 1)

            def latent_mean_squares(L, i):
                n = (QR, KVR)[i]
                dve.wait_ge(lat_sq.sem, lat_sq.upto(L, 2 * i + 2))
                dve.tensor_scalar(stat[:, LMS + 2 * i:LMS + 2 * i + 2], stat[:, LSQ + 2 * i:LSQ + 2 * i + 2],
                                  1.0 / n, EPS, ALU.mult, ALU.add).then_inc(lat_ms.sem, 1)

            def rotate_key(L):
                h = ROPE // 2
                k = psum[:, 2:4, KVR:KVR + ROPE]
                times(rot_a, k, rot_t[:, :, 0, :])
                times(rot_b[:, :, 0:h], k[:, :, h:], rot_t[:, :, 1, 0:h])
                times(rot_b[:, :, h:], k[:, :, 0:h], rot_t[:, :, 1, h:]).then_inc(krot_step.sem, 1)
                dve.wait_ge(krot_step.sem, krot_step.upto(L, 1))
                for i in range(2):
                    dve.tensor_tensor(kvlat_s[:, :, KVR + i * ROPE:KVR + (i + 1) * ROPE], rot_a, rot_b,
                                      ALU.add).then_inc(krot_step.sem, 1)

            def latent(L, i):
                for t in range(TB):
                    low(L, lat_hi, 2 * i + t + 1, latT[:, 1, 3 * i:3 * i + 3, blk(t)],
                        psum[:, (4, 2)[i] + t, 0:3 * P].rearrange("p (k n) -> p k n", k=3),
                        latT[:, 0, 3 * i:3 * i + 3, blk(t)], lat_lo)

            def pool_scale_rows(L, i):
                products(dve, L, pool_done, 0, i, MIX0 + M_MAPS)
                src = banks(6)
                if i == 0:
                    last = times(tmp, src, inv_count[:, :])
                else:
                    scale = pscale[:, bass.ds(L, 1), :].rearrange("p l g -> p (l g)")
                    last = dve.tensor_tensor(tmp.rearrange("p (g n) -> p g n", g=PG),
                                             src.rearrange("p (g n) -> p g n", g=PG),
                                             scale.unsqueeze(2).to_broadcast([P, PG, S]), ALU.mult)
                last.then_inc(pool_scaled.sem, 1)

            def pool_low(L, i):
                dst = (poolT, mixT)[i]
                low(L, pool_hi, i + 1, flat(dst, 1), tmp, flat(dst, 0), pool_lo)

            def parts(L, p, which):
                for part in which:
                    src = psum[:, 2 + part, :]
                    if part == QRO:
                        part_products(dve, L, p, part)
                        both = src.rearrange("p (h n) -> p h n", h=2)
                        times(both, both, rot_f.unsqueeze(1).to_broadcast([P, 2, S])).then_inc(rope_done.sem, 1)
                    low(L, part_hi, 4 * p + part + 1, flat(pair(p, part), 1), src, flat(pair(p, part), 0), part_lo)

            def mask_and_max(L, p):
                row, st = scores[:, p % 2, :], stat2[:, p % 2, :]
                two = lambda v: v.rearrange("p (h n) -> p h n", h=2)
                dve.wait_ge(score_done.sem, score_done.upto(L, p + 1))
                dve.tensor_tensor(two(row[:, 0:2 * S]), two(psum[:, 6, :]),
                                  causal[:, :].unsqueeze(1).to_broadcast([P, 2, S]), ALU.add)
                dve.tensor_tensor(two(row[:, 2 * S:3 * S]), two(psum[:, 7, 0:S]),
                                  causal[:, P:].unsqueeze(1).to_broadcast([P, 2, P]), ALU.add).then_inc(score_masked.sem, 1)
                dve.wait_ge(score_masked.sem, score_masked.upto(L, p + 1))
                dve.tensor_reduce(st[:, 0:2], two(row[:, 0:2 * S]), AX.X, ALU.max)
                dve.tensor_reduce(st[:, 2:4], two(row[:, 2 * S:3 * S]), AX.X, ALU.max).then_inc(max_done.sem, 1)
                dve.wait_ge(max_done.sem, max_done.upto(L, p + 1))
                dve.tensor_scalar(st[:, 4:8], st[:, 0:4], -SCALE, None, ALU.mult).then_inc(bias_done.sem, 1)

            def normalise(L, p):
                row, st = scores[:, p % 2, :], stat2[:, p % 2, :]
                dve.wait_ge(exp_done.sem, exp_done.upto(L, p + 1))
                dve.reciprocal(st[:, 12:16], st[:, 8:12]).then_inc(inv_done.sem, 1)
                dve.wait_ge(inv_done.sem, inv_done.upto(L, p + 1))
                for cols, i, n in ((slice(0, 2 * S), 12, S), (slice(2 * S, 3 * S), 14, P)):
                    v = row[:, cols].rearrange("p (h n) -> p h n", h=2)
                    last = times(v, v, st[:, i:i + 2].unsqueeze(2).to_broadcast([P, 2, n]))
                last.then_inc(prob_done.sem, 1)

            def probs(L, p):
                low(L, prob_hi, p + 1, small_T[:, 1, 0:3 * S], banks(0)[:, 0:3 * S], small_T[:, 0, 0:3 * S], prob_lo)

            def heads_out(L, p):
                o = oT[:, :, 2 * p:2 * p + 2, :]
                low(L, o_hi, p + 1, flat(o, 1), psum[:, 0, :], flat(o, 0), o_lo)

            def gate_a(L, n):
                for t in range(TB):
                    g = gates[:, t, n * N512:(n + 1) * N512]
                    products(dve, L, a_done, n, t, MIX0 + M_PP + n)
                    times(g, g, psum[:, 2 + 2 * n + t, :]).then_inc(a_gated.sem, 1)

            def gate_b(L, n):
                for t in range(TB):
                    cols = slice(n * N512, (n + 1) * N512)
                    products(dve, L, b_done, n, t, MIX0 + M_AP + 2 * n + 1)
                    times(xs[:, t, cols], gates[:, t, D + n * N512:D + (n + 1) * N512],
                          psum[:, 2 + 2 * n + t, :]).then_inc(b_gated.sem, 1)
                    dve.wait_ge(b_gated.sem, b_gated.upto(L, TB * n + t + 1))
                    dve.tensor_tensor(xs[:, t, cols], xs[:, t, cols], gates[:, t, cols], ALU.add).then_inc(merged.sem, 1)

            def mixer(L):
                split_mix(L, 2)
                split_mix(L, 3)
                latent_mean_squares(L, 0)
                split_mix(L, 4)
                latent_norm(L, 0)
                split_mix(L, 5)
                latent_mean_squares(L, 1)
                split_mix(L, 6)
                latent_norm(L, 1)
                rotate_key(L)
                split_mix(L, 7)
                for t in range(TB):
                    low(L, xp_hi, t + 1, xpt[:, 1, t, :], psum[:, 6 + t, :], xpt[:, 0, t, :], xp_lo)
                split_mix(L, 8)
                split_mix(L, 9)
                gate(L, 0)
                latent(L, 0)
                split_mix(L, 10)
                split_mix(L, 11)
                gate(L, 1)
                latent(L, 1)
                pool_scale_rows(L, 0)
                pool_low(L, 0)
                split_mix(L, 12)
                split_mix(L, 13)
                gate(L, 2)
                split_mix(L, 14)
                pool_scale_rows(L, 1)
                pool_low(L, 1)
                split_mix(L, 15)
                split_mix(L, 16)
                gate(L, 3)
                split_mix(L, 17)
                parts(L, 0, (QN, QRO))
                split_mix(L, 18)
                parts(L, 0, (KN, VV))
                split_mix(L, 19)
                parts(L, 1, (QN, QRO))
                split_mix(L, 20)
                parts(L, 1, (KN, VV))
                mask_and_max(L, 0)
                split_mix(L, 21)
                parts(L, 2, (QN, QRO))
                split_mix(L, 22)
                normalise(L, 0)
                parts(L, 2, (KN,))
                probs(L, 0)
                mask_and_max(L, 1)
                heads_out(L, 0)
                parts(L, 2, (VV,))
                split_mix(L, 23)
                parts(L, 3, (QN, QRO))
                split_mix(L, 24)
                normalise(L, 1)
                parts(L, 3, (KN,))
                probs(L, 1)
                mask_and_max(L, 2)
                heads_out(L, 1)
                parts(L, 3, (VV,))
                split_mix(L, 25)
                normalise(L, 2)
                probs(L, 2)
                mask_and_max(L, 3)
                dve.wait_ge(gate_sig.sem, gate_sig.upto(L, 4 * TB))
                gate_a(L, 0)
                heads_out(L, 2)
                split_mix(L, 26)
                normalise(L, 3)
                gate_a(L, 1)
                probs(L, 3)
                split_mix(L, 27)
                heads_out(L, 3)
                split_mix(L, 28)
                gate_b(L, 0)
                split_mix(L, 29)
                split_mix(L, 30)
                gate_b(L, 1)
                for t in range(TB):
                    low(L, mrg_hi, t + 1, xT[:, 1, :, blk(t)],
                        banks(MERGE_T_BANK[t]).rearrange("p (k n) -> p k n", k=KD), xT[:, 0, :, blk(t)], mrg_lo)
                for m in range(31, 35):
                    split_mix(L, m)
                for t in range(TB):
                    products(dve, L, y_done, 1, t, MIX0 + MIX_GROUPS - 1)
                    dve.tensor_tensor(x[:, t, :], banks(2 * t), x[:, t, :], ALU.add).then_inc(x_ready.sem, 1)

            dve.sem_inc(w_lo_done.sem, RING)
            rotary_setup()
            dve.wait_ge(x_landed, 16)
            dve.sem_inc(x_ready.sem, TB)
            with nc.vector.Fori(0, DEPTH) as L:
                def first_groups():
                    split(L, 0, 0)
                    split(L, 0, 1)
                norm(L, 0, first_groups)
                ffn(L, 0)
                norm(L, 1, lambda: split_mix(L, 1))
                mixer(L)
                norm(L, 2, lambda: None)
                ffn(L, 1)
            for t in range(TB):
                mean_squares(DEPTH, 0, t)
            for t in range(TB):
                scale_rows(DEPTH, 0, t)

        @block.tensor
        def _(pe):
            def passes(dst, a_hi, a_lo, b_hi, b_lo, first, last):
                nc.tensor.matmul(dst, a_hi, b_hi, start=first, stop=False)
                nc.tensor.matmul(dst, a_hi, b_lo, start=False, stop=False)
                return nc.tensor.matmul(dst, a_lo, b_hi, start=False, stop=last)

            def wait(ev, L, n):
                pe.wait_ge(ev.sem, ev.upto(L, n))

            def weights(L, q, r):
                wait(w_lo_done, L, RING * q + r + 1)
                return w_hi[:, r, :], w_lo[:, r, :]

            def mix_weights(L, m):
                return weights(L, (MIX0 + m) // RING, m % RING)

            def tiles(dst, src, count, done=None):
                for k in range(count):
                    last = nc.tensor.transpose(dst[:, k * P:(k + 1) * P], src[:, k * P:(k + 1) * P], ident[:, :])
                if done is not None:
                    last.then_inc(done.sem, 1)
                return last

            def norm(L, s):
                for t in range(TB):
                    wait(normed, L, TB * s + t + 1)
                    tiles(banks(NORM_T_BANK[t]), xs[:, t, :], KD, norm_tr)

            def project(w, width, bank, a, stat_T, halves, done=None):
                hi, lo = w
                for t in range(TB):
                    for k in range(4):
                        cols = slice(k * width, (k + 1) * width)
                        last = passes(psum[:, bank[t], 0:width], stat_T[:, 0, 4 * a + k, blk(t)],
                                      stat_T[:, 1, 4 * a + k, blk(t)], hi[:, cols], lo[:, cols],
                                      first=(a == 0 and k == 0), last=(a == halves - 1 and k == 3))
                    if t == 0 and done is not None:
                        last.then_inc(done.sem, 1)
                last.then_inc(w_used.sem, 1)

            def turn_hidden(L, f, j):
                for t in range(TB):
                    wait(act_done, L, (f * NCH + j) * TB + t + 1)
                    for k in range(KCH):
                        last = nc.tensor.transpose(psum[:, TR_BANK, k * S + t * P:k * S + (t + 1) * P],
                                                   act_sb[:, t, k * P:(k + 1) * P], ident[:, :])
                last.then_inc(hid_tr.sem, 1)

            def down(L, f, q, r, j, between=None):
                hi, lo = weights(L, q, r)
                at = hid_cols(j).start
                wait(hid_lo, L, f * NCH + j + 1)
                first, final = isinstance(j, int) and j == 0, isinstance(j, int) and j == NCH - 1
                for t in range(TB):
                    if t == 1 and between is not None:
                        between()
                    for n in range(2):
                        for k in range(KCH):
                            cols = slice(k * D + n * N512, k * D + (n + 1) * N512)
                            tile = slice(at + k * S + t * P, at + k * S + (t + 1) * P)
                            last = passes(psum[:, 2 * t + n, :], small_T[:, 0, tile], small_T[:, 1, tile],
                                          hi[:, cols], lo[:, cols], first=(first and k == 0),
                                          last=(final and k == KCH - 1))
                    if final and t == 0:
                        last.then_inc(y_done.sem, 1)
                last.then_inc(w_used.sem, 1)

            def ffn(L, f):
                q0 = f * FFN2_0 // RING
                gu = (GU_BANK, GU_BANK + 1)
                wait(norm_lo, L, 2 * TB * f + TB)
                project(weights(L, q0, 0), N512, gu, 0, xT, 2)
                project(weights(L, q0, 1), N512, gu, 1, xT, 2, gu_done)

                def chunk(j, first=False, between=None):
                    w = weights(L, q0 + j - 1, 2)
                    wait(act_done, L, (f * NCH + j) * TB)
                    project(w, N512, gu, 0, xT, 2)
                    turn_hidden(L, f, j - 1)
                    project(weights(L, q0 + j, 0), N512, gu, 1, xT, 2, gu_done)
                    down(L, f, q0 + j, 1, j - 1, between)

                chunk(1)
                with nc.tensor.Fori(2, NCH - 1) as j:
                    chunk(j)
                chunk(NCH - 1, between=lambda: turn_hidden(L, f, NCH - 1))
                down(L, f, q0 + NCH - 1, 2, NCH - 1)

            def pair_parts(L, p):
                def free(part):
                    if p:
                        wait(part_lo, L, 4 * (p - 1) + part + 1)

                hi, lo = mix_weights(L, M_PAIR + 2 * p)
                for part, tile0 in ((QN, 0), (QRO, 2)):
                    free(part)
                    for i in range(2):
                        for k in range(3):
                            cols = slice(k * N512 + (tile0 + i) * P, k * N512 + (tile0 + i + 1) * P)
                            last = passes(psum[:, 2 + part, i * S:(i + 1) * S], hi[:, cols], lo[:, cols],
                                          qlT[:, 0, k, :], qlT[:, 1, k, :], first=(k == 0), last=(k == 2))
                    if part == QN:
                        last.then_inc(part_done.sem, 1)
                last.then_inc(w_used.sem, 1)
                hi, lo = mix_weights(L, M_PAIR + 2 * p + 1)
                free(KN)
                for i in range(2):
                    for k in range(2):
                        cols = slice(k * N512 + i * 2 * P, k * N512 + i * 2 * P + P)
                        last = passes(psum[:, 2 + KN, i * S:(i + 1) * S], hi[:, cols], lo[:, cols],
                                      kvT[:, 0, k, :], kvT[:, 1, k, :], first=(k == 0), last=(k == 1))
                last.then_inc(part_done.sem, 1)
                free(VV)
                def values(w, k):
                    return w[:, k * N512:(k + 1) * N512].rearrange("p (h c n) -> p h c n", h=2, c=2)[:, :, 1, :]
                for t in range(TB):
                    for k in range(2):
                        last = passes(psum[:, 2 + VV, t * S:(t + 1) * S].rearrange("p (h n) -> p h n", h=2),
                                      kvT[:, 0, k, blk(t)], kvT[:, 1, k, blk(t)],
                                      values(hi, k), values(lo, k), first=(k == 0), last=(k == 1))
                last.then_inc(w_used.sem, 1)

            def pair_scores(L, p):
                wait(part_lo, L, 4 * p + 4)
                if p:
                    wait(score_masked, L, p)
                else:
                    wait(pool_scaled, L, 2)
                q, qr, k = pair(p, QN), pair(p, QRO), pair(p, KN)
                for t, bank, n in ((1, 6, S), (0, 7, P)):
                    for i in range(2):
                        dst = psum[:, bank, i * n:(i + 1) * n]
                        passes(dst, q[:, 0, i, blk(t)], q[:, 1, i, blk(t)], k[:, 0, i, 0:n], k[:, 1, i, 0:n],
                               first=True, last=False)
                        last = passes(dst, qr[:, 0, i, blk(t)], qr[:, 1, i, blk(t)], krT[:, 0, 0:n], krT[:, 1, 0:n],
                                      first=False, last=True)
                last.then_inc(score_done.sem, 1)

            def turn_probs(L, p):
                wait(prob_done, L, p + 1)
                if p:
                    wait(o_lo, L, p)
                row = scores[:, p % 2, :]
                for i in range(2):
                    for dst, src in ((psum[:, 0, i * S:i * S + P], 2 * S + i * P),
                                     (psum[:, 0, i * S + P:(i + 1) * S], i * S),
                                     (psum[:, 1, i * P:(i + 1) * P], i * S + P)):
                        last = nc.tensor.transpose(dst, row[:, src:src + P], ident[:, :])
                last.then_inc(prob_tr.sem, 1)

            def pair_values(L, p):
                wait(prob_lo, L, p + 1)
                v = pair(p, VV)
                for i in range(2):
                    c = slice(i * P, (i + 1) * P)
                    passes(psum[:, 0, i * S:(i + 1) * S], v[:, 0, 0, c], v[:, 1, 0, c],
                           small_T[:, 0, i * S:(i + 1) * S], small_T[:, 1, i * S:(i + 1) * S], first=True, last=False)
                    late = slice(2 * S + i * P, 2 * S + (i + 1) * P)
                    last = passes(psum[:, 0, i * S + P:(i + 1) * S], v[:, 0, 1, c], v[:, 1, 1, c],
                                  small_T[:, 0, late], small_T[:, 1, late], first=False, last=True)
                last.then_inc(pv_done.sem, 1)

            def latent(L, i):
                bank, src = ((4, qlat_s), (2, kvlat_s))[i]
                wait(lat_normed, L, i + 1)
                if i:
                    wait(krot_step, L, 3)
                for t in range(TB):
                    tiles(psum[:, bank + t, :], src[:, t, :], 3, lat_tr)

            def window_sums(L):
                wait(xp_lo, L, TB)
                for g in range(PG):
                    dst = psum[:, 6 + g // 2, (g % 2) * S:(g % 2 + 1) * S]
                    c = slice(g * P, (g + 1) * P)
                    early, late = window[:, g * S:(g + 1) * S], window[:, PG * S + g * P:PG * S + (g + 1) * P]
                    for i in range(2):
                        nc.tensor.matmul(dst, xpt[:, i, 0, c], early, start=(i == 0), stop=False)
                    for i in range(2):
                        last = nc.tensor.matmul(dst[:, P:], xpt[:, i, 1, c], late, start=False, stop=(i == 1))
                last.then_inc(pool_done.sem, 1)

            def pool_mix(L):
                hi, lo = mix_weights(L, M_MAPS)
                wait(pool_lo, L, 1)
                for g in range(PG):
                    c = slice(g * P, (g + 1) * P)
                    last = passes(psum[:, 6 + g // 2, (g % 2) * S:(g % 2 + 1) * S], hi[:, c], lo[:, c],
                                  poolT[:, 0, g, :], poolT[:, 1, g, :], first=True, last=True)
                last.then_inc(w_used.sem, 1)

            def gate(L, c, m):
                project(mix_weights(L, m), N512, (0, 1), 0, xT, 2)
                project(mix_weights(L, m + 1), N512, (0, 1), 1, xT, 2, gate_done)

            def mixer(L):
                wait(norm_lo, L, 2 * TB)
                project(mix_weights(L, M_Q), QR, (4, 5), 0, xT, 2)
                project(mix_weights(L, M_Q + 1), QR, (4, 5), 1, xT, 2, q_done)
                project(mix_weights(L, M_KV), KVW, (2, 3), 0, xT, 2)
                project(mix_weights(L, M_KV + 1), KVW, (2, 3), 1, xT, 2, kv_done)
                project(mix_weights(L, M_POOL), POOL, (6, 7), 0, xT, 2)
                project(mix_weights(L, M_POOL + 1), POOL, (6, 7), 1, xT, 2, xp_done)
                gate(L, 0, M_G0)
                latent(L, 0)
                wait(gate_biased, L, TB)
                gate(L, 1, M_G1)
                latent(L, 1)
                window_sums(L)
                wait(gate_biased, L, 2 * TB)
                gate(L, 2, M_G2)
                pool_mix(L)
                wait(gate_biased, L, 3 * TB)
                gate(L, 3, M_G3)
                wait(lat_lo, L, 2 * TB)
                pair_parts(L, 0)
                pair_parts(L, 1)
                pair_scores(L, 0)
                pair_parts(L, 2)
                wait(gate_biased, L, 4 * TB)
                turn_probs(L, 0)
                pair_scores(L, 1)
                pair_values(L, 0)
                pair_parts(L, 3)
                turn_probs(L, 1)
                pair_scores(L, 2)
                pair_values(L, 1)
                w = mix_weights(L, M_PP)
                wait(part_lo, L, 4 * PAIRS)
                wait(pool_lo, L, 2)
                project(w, N512, (2, 3), 0, mixT, 1, a_done)
                turn_probs(L, 2)
                pair_scores(L, 3)
                pair_values(L, 2)
                project(mix_weights(L, M_PP + 1), N512, (4, 5), 0, mixT, 1, a_done)
                turn_probs(L, 3)
                w = mix_weights(L, M_AP)
                wait(a_gated, L, TB)
                wait(o_lo, L, 2)
                project(w, N512, (2, 3), 0, oT, 2)
                pair_values(L, 3)
                w = mix_weights(L, M_AP + 1)
                wait(o_lo, L, PAIRS)
                project(w, N512, (2, 3), 1, oT, 2, b_done)
                w = mix_weights(L, M_AP + 2)
                wait(a_gated, L, 2 * TB)
                project(w, N512, (4, 5), 0, oT, 2)
                project(mix_weights(L, M_AP + 3), N512, (4, 5), 1, oT, 2, b_done)
                for t in range(TB):
                    wait(merged, L, TB + t + 1)
                    tiles(banks(MERGE_T_BANK[t]), xs[:, t, :], KD, mrg_tr)
                wait(mrg_lo, L, TB)
                for n in range(2):
                    project(mix_weights(L, M_WO + 2 * n), N512, (n, 2 + n), 0, xT, 2)
                    project(mix_weights(L, M_WO + 2 * n + 1), N512, (n, 2 + n), 1, xT, 2, y_done if n else None)

            pe.sem_inc(w_used.sem, RING)
            pe.wait_ge(const_landed, 16 * 5)
            pe.wait_ge(setup_done, 2)
            with nc.tensor.Fori(0, DEPTH) as L:
                norm(L, 0)
                ffn(L, 0)
                norm(L, 1)
                mixer(L)
                norm(L, 2)
                ffn(L, 1)


_CONSTANTS = ("c_ident", "c_causal", "c_window", "c_inv_count", "c_rotary")
_INS = ("ffn1_up", "ffn1_down", "w_in", "b_gate", "pool_maps", "pool_scale", "w_pool_proj", "q_latent_norm",
        "w_uq", "kv_latent_norm", "w_ukv", "w_attn_proj", "w_out", "ffn2_up", "ffn2_down")


def kernel(**inputs):
    import concourse.bacc as _bacc
    from concourse.bass_utils import run_bass_kernel_spmd as _run

    nc = _bacc.Bacc("TRN2", target_bir_lowering=False, num_devices=1)
    arrays = {name: np.ascontiguousarray(inputs[name]) for name in ("x", "positions") + _INS}
    rows = [inputs[name][layer] for layer in range(DEPTH) for name in ("norm_ffn1", "norm_mix", "norm_ffn2")]
    arrays["gains"] = np.ascontiguousarray(np.stack(rows + [inputs["final_norm"]]))
    arrays.update(shape_constants())
    names = ("x", "positions", "gains") + _INS + _CONSTANTS
    args = [nc.dram_tensor(name + "_dram", arrays[name].shape, mybir.dt.from_np(arrays[name].dtype),
                           kind="ExternalInput").ap() for name in names]
    out = nc.dram_tensor("out_dram", arrays["x"].shape, F32, kind="ExternalOutput").ap()
    trunk(nc, *args, out)
    r = _run(nc, [{name + "_dram": arrays[name] for name in names}], core_ids=[0])
    return r.results[0]["out_dram"]
```

```python
import numpy as np
from contextlib import ExitStack

import concourse.bass as bass
from concourse import mybir

F32 = mybir.dt.float32
F32R = mybir.dt.float32r
I32 = mybir.dt.int32
ACT = mybir.ActivationFunctionType
ALU = mybir.AluOpType
AX = mybir.AxisListType

P = 128
S, D, DEPTH = 256, 1024, 2
TB = S // P
KD = D // P
HEADS, NOPE, ROPE, VD = 8, 128, 64, 128
QK = NOPE + ROPE
QR, KVR = 384, 256
WINDOWS = (2, 4, 8, 16)
PG = len(WINDOWS)
RAMP = max(WINDOWS)
POOL = PG * P
FF = 2816
EPS = 1e-6
THETA = 10000.0
SCALE = float(QK) ** -0.5
MASKED = -1e30

CH = 256
NCH = FF // CH
KCH = CH // P
GROUP = 2048
RING = 3
N512 = 512
PAIRS = HEADS // 2

C_POOL, C_Q, C_KV, C_GATE = 0, POOL, POOL + QR, POOL + QR + KVR + ROPE
KVW = KVR + ROPE

FFN_GROUPS = 3 * NCH
M_Q, M_KV, M_POOL, M_G0, M_G1, M_G2, M_MAPS, M_G3 = 0, 2, 4, 6, 8, 10, 12, 13
M_PAIR = 15
M_PP = M_PAIR + 2 * PAIRS
M_AP = M_PP + 2
M_WO = M_AP + 4
MIX_GROUPS = M_WO + 4
MIX0 = FFN_GROUPS
FFN2_0 = FFN_GROUPS + MIX_GROUPS
GROUPS = 2 * FFN_GROUPS + MIX_GROUPS
UPS = (NCH, 1, NCH - 1)
assert GROUPS % RING == 0 and FFN2_0 % RING == 0 and FFN_GROUPS % RING == 0

ROUND = 1.5 * 2.0 ** 23
TWO_PI = (6.28125, float(np.float32(0.0019350051879882812)), 3.0199159819344e-07)
PI_LOW = float(np.nextafter(np.float32(np.pi), np.float32(0)))

ROT_STEPS = 5 + TB + 2 * 8 + 6

QN, QRO, KN, VV = range(4)
PART_ORDER = [(p, part) for p in range(2) for part in (QN, QRO, KN, VV)]
PART_ORDER += [(2, QN), (2, QRO), (2, KN), (3, QN), (3, QRO), (2, VV), (3, KN), (3, VV)]

GU_BANK, TR_BANK = 4, 6
NORM_T_BANK = ((6, 7), (0, 2))
MERGE_T_BANK = ((6, 7), (3, 1))


def shape_constants():
    ident = np.eye(P, dtype=np.float32)
    causal = np.where(np.arange(P)[:, None] >= np.arange(P)[None, :], 0.0, MASKED).astype(np.float32)
    t = np.arange(S)
    window = np.zeros((S, PG, S), np.float32)
    inv_count = np.zeros((PG, S), np.float32)
    for g, w in enumerate(WINDOWS):
        inside = (t[:, None] <= t[None, :]) & (t[:, None] > t[None, :] - w)
        count = np.minimum(t + 1, w)
        window[:, g] = inside - np.eye(S) * count[None, :]
        inv_count[g] = np.float32(1.0) / count.astype(np.float32)
    window = np.concatenate([window[:P].reshape(P, -1), window[P:, :, P:].reshape(P, -1)], axis=1)
    half = ROPE // 2
    freq = np.float32(THETA) ** (-np.arange(0, ROPE, 2, dtype=np.float32) / np.float32(ROPE))
    freq = freq.astype(np.float32)
    quarter = np.float32(np.pi / 2)
    freq_f = np.tile(freq, 4)[:, None] * np.ones((1, S), np.float32)
    phase_f = np.repeat([quarter, quarter, 0, 0], half)[:, None] * np.ones((1, S), np.float32)
    sign_f = np.repeat([1, 1, -1, 1], half)[:, None] * np.ones((1, S), np.float32)
    freq_t = np.tile(freq, 4 * TB)[None] * np.ones((P, 1), np.float32)
    phase_t = np.tile(np.repeat([quarter, quarter, 0, 0], half), TB)[None] * np.ones((P, 1), np.float32)
    sign_t = np.tile(np.repeat([1, 1, -1, 1], half), TB)[None] * np.ones((P, 1), np.float32)
    rotary = np.stack([np.concatenate([a, b], axis=1) for a, b in
                       ((freq_f, freq_t), (phase_f, phase_t), (sign_f, sign_t))], axis=1)
    return {
        "c_ident": ident, "c_causal": causal, "c_window": window.astype(np.float32),
        "c_inv_count": np.ascontiguousarray(inv_count[None, :, :RAMP]), "c_rotary": rotary.astype(np.float32),
    }


class Event:

    def __init__(self, sem, per_layer, first=0):
        self.sem, self.per_layer, self.first = sem, per_layer, first

    def upto(self, layer, n):
        return layer * self.per_layer + (n + self.first)


def trunk(nc, x_in, positions, gains, ffn1_up, ffn1_down, w_in, b_gate, pool_maps, pool_scale,
          w_pool_proj, q_latent_norm, w_uq, kv_latent_norm, w_ukv, w_attn_proj, w_out,
          ffn2_up, ffn2_down, c_ident, c_causal, c_window, c_inv_count, c_rotary, out):
    with ExitStack() as ctx:
        def sb(name, shape, dt=F32):
            return ctx.enter_context(nc.sbuf_tensor(name, shape, dt))

        def sem(name):
            return ctx.enter_context(nc.semaphore(name))

        def event(name, per_layer, first=0):
            return Event(sem(name), per_layer, first)

        x = sb("x", [P, TB, D])
        xs = sb("xs", [P, TB, D])
        raw = sb("raw", [P, RING, GROUP])
        w_hi = sb("w_hi", [P, RING, GROUP], F32R)
        w_lo = sb("w_lo", [P, RING, GROUP], F32R)
        xT = sb("xT", [P, 2, KD, S], F32R)
        pair1 = sb("pair1", [P, 2, KD, S], F32R)
        small_T = sb("small_T", [P, 2, 4 * S], F32R)
        latT = sb("latT", [P, 2, 3 + 3, S], F32R)
        oT = sb("oT", [P, 2, HEADS, S], F32R)
        xp = sb("xp", [P, 2, PG * S], F32R)
        window = sb("window", [P, PG * (S + P)], F32R)
        gates = sb("gates", [P, TB, 2 * D])
        scores = sb("scores", [P, 2, 3 * S])
        ident = sb("ident", [P, P])
        ident_r = sb("ident_r", [P, P], F32R)
        causal_r = sb("causal_r", [P, P], F32R)
        inv_count = sb("inv_count", [P, PG, RAMP])
        gain = sb("gain", [P, D])
        lat_gain = sb("lat_gain", [P, QR + KVR])
        angle = sb("angle", [P, 2 * S])
        rot = sb("rot", [P, 2 * S])
        pscale = sb("pscale", [P, DEPTH, PG])
        stat = sb("stat", [P, 32])
        psum = ctx.enter_context(nc.psum_tensor("psum", [P, 8, N512], F32))

        silu_sb = scores[:, 0, 0:TB * CH].rearrange("p (t n) -> p t n", t=TB)
        act_sb = scores[:, 1, 0:TB * CH].rearrange("p (t n) -> p t n", t=TB)
        tmp = scores[:, :, :].rearrange("p a n -> p (a n)")[:, 0:PG * S]
        poolT = oT[:, :, 0:PG, :]
        mixT = xp[:, :, :].rearrange("p s (g t) -> p s g t", g=PG)
        xpt = xp[:, :, :].rearrange("p s (t n) -> p s t n", t=TB)
        qlat_s = xs[:, 0, 0:TB * QR].rearrange("p (t n) -> p t n", t=TB)
        kvlat_s = xs[:, 1, 0:TB * 3 * P].rearrange("p (t n) -> p t n", t=TB)
        rot_a = xs[:, 1, 3 * S:3 * S + TB * ROPE].rearrange("p (t n) -> p t n", t=TB)
        rot_b = xs[:, 1, 3 * S + TB * ROPE:3 * S + 2 * TB * ROPE].rearrange("p (t n) -> p t n", t=TB)
        qlT, kvT, krT = latT[:, :, 0:3, :], latT[:, :, 3:5, :], latT[:, :, 5, :]
        rot_f = rot[:, 0:S]
        rot_t = rot[:, S:2 * S].rearrange("p (t c n) -> p t c n", t=TB, c=2)

        def pair(p, part):
            buf = (xT, pair1)[p % 2]
            return buf[:, :, 2 * part:2 * part + 2, :]

        NSQ, NMS, NRS = 0, 2, 4
        LSQ, LMS, LRS = 6, 10, 14
        SMX, SNM, SSUM, SINV = 18, 22, 26, 28
        stat2 = sb("stat2", [P, 2, 16])
        half_neg, neg_one = sb("half_neg", [P, 2]), sb("neg_one", [P, 4])
        table_junk = sb("table_junk", [P, 1])
        pos_col_i, pos_col = sb("pos_col_i", [P, TB], I32), sb("pos_col", [P, TB])
        rotary = gates[:, 0, 0:6 * S].rearrange("p (c n) -> p c n", c=3)
        freq, phase, sign = (rotary[:, i, :] for i in range(3))
        pos_row_i = gates[:, 0, 6 * S:7 * S].bitcast(I32)
        pos_row = gates[:, 0, 7 * S:8 * S]
        product = gates[:, 0, 6 * S:8 * S]
        turns = gates[:, 1, 0:2 * S]
        causal_f = turns[:, 0:P]
        window_f = gates[:, 1, 2 * S:8 * S]
        square_junk = scores[:, :, :].rearrange("p a n -> p (a n)")[:, 0:D]
        ROWS = (slice(0, S), slice(S, 2 * S), slice(2 * S, 2 * S + P), slice(2 * S + P, 3 * S))

        loads_begun = sem("loads_begun")
        raw_landed = [sem(f"raw_landed{i}") for i in range(RING)]
        x_landed = [sem(f"x_landed{t}") for t in range(TB)]
        ident_landed, gain0_landed = sem("ident_landed"), sem("gain0_landed")
        const_landed, out_landed = sem("const_landed"), sem("out_landed")
        gain_landed, latg_landed, bias_landed = sem("gain_landed"), sem("latg_landed"), sem("bias_landed")
        w_hi_done = event("w_hi_done", GROUPS)
        w_lo_done = event("w_lo_done", GROUPS, RING)
        w_lo_half = event("w_lo_half", 1)
        w_used = event("w_used", GROUPS, RING)
        exponent_set, pos_landed = sem("exponent_set"), sem("pos_landed")
        out_rows = sem("out_rows")
        rot_step, rotary_ready = sem("rot_step"), event("rotary_ready", 1)
        QUARTERS = 2 * TB
        x_ready = event("x_ready", 3 * QUARTERS, QUARTERS)
        normed = [event(f"normed{h}", 3 * TB, TB) for h in range(2)]
        norm_tr = event("norm_tr", 3 * QUARTERS, QUARTERS)
        norm_hi = event("norm_hi", 3 * QUARTERS, QUARTERS)
        norm_lo = event("norm_lo", 3 * QUARTERS, QUARTERS)
        sq_done = event("sq_done", 3 * TB)
        ms_done = event("ms_done", 3 * TB)
        rstd_done = event("rstd_done", 3 * TB)
        gu_done = event("gu_done", 2 * NCH)
        silu_done = event("silu_done", 2 * NCH * TB)
        act_done = event("act_done", 2 * NCH * TB)
        hid_tr = event("hid_tr", 2 * NCH)
        hid_hi = event("hid_hi", 2 * NCH)
        hid_lo = event("hid_lo", 2 * NCH)
        y_done = event("y_done", 3 + 2 + 3)
        q_done, kv_done, xp_done = event("q_done", 1), event("kv_done", 1), event("xp_done", 1)
        lat_sq = event("lat_sq", 2 * TB)
        lat_ms = event("lat_ms", 2)
        lat_rstd, lat_scale = event("lat_rstd", 2), event("lat_scale", 2)
        lat_normed = event("lat_normed", 2)
        krot_step = event("krot_step", 4)
        lat_tr, lat_hi, lat_lo = event("lat_tr", 2 * TB), event("lat_hi", 2 * TB), event("lat_lo", 2 * TB)
        xp_hi, xp_lo = event("xp_hi", TB), event("xp_lo", TB)
        gate_done, gate_biased, gate_sig = event("gate_done", 4), event("gate_biased", 4 * TB), event("gate_sig", 4 * TB)
        pool_done, pool_scaled = event("pool_done", 1), event("pool_scaled", 2)
        pool_hi, pool_lo = event("pool_hi", 2), event("pool_lo", 2)
        part_done = event("part_done", 2 * PAIRS)
        rope_done = event("rope_done", PAIRS)
        part_hi, part_lo = event("part_hi", 4 * PAIRS), event("part_lo", 4 * PAIRS)
        score_done = event("score_done", PAIRS)
        max_done, bias_done, exp_done = event("max_done", PAIRS), event("bias_done", PAIRS), event("exp_done", PAIRS)
        inv_done, prob_done = event("inv_done", PAIRS), event("prob_done", PAIRS)
        prob_tr, prob_hi, prob_lo = event("prob_tr", PAIRS), event("prob_hi", PAIRS), event("prob_lo", PAIRS)
        pv_done, o_hi, o_lo = event("pv_done", PAIRS), event("o_hi", PAIRS), event("o_lo", PAIRS)
        a_done, a_gated = event("a_done", 2), event("a_gated", 2 * TB)
        b_done, b_gated, merged = event("b_done", 2), event("b_gated", 2 * TB), event("merged", 2 * TB)
        mrg_tr, mrg_hi, mrg_lo = event("mrg_tr", 2 * TB), event("mrg_hi", 2 * TB), event("mrg_lo", 2 * TB)

        ups, downs = (ffn1_up, ffn2_up), (ffn1_down, ffn2_down)

        def blk(t):
            return slice(t * P, (t + 1) * P)

        def flat(v, i):
            return v[:, i].rearrange("p a n -> p (a n)")

        def products(eng, L, ev, i, t, g):
            if t == 0:
                eng.wait_ge(ev.sem, ev.upto(L, i + 1))
            else:
                eng.wait_ge(w_used.sem, w_used.upto(L, g + 1))

        def quarter(s, h, t):
            return QUARTERS * (s - 1) + TB * h + t + 1

        def normed_count(s, t):
            return TB * (s - 1) + t + 1

        def half(h):
            return slice(h * N512, (h + 1) * N512)

        def part_count(p, part):
            return PART_ORDER.index((p, part)) + 1

        def y_ready(eng, L, s, h, t):
            n = TB * h + t
            if s != 2:
                g = FFN_GROUPS if s == 1 else GROUPS
                if n == 3:
                    eng.wait_ge(w_used.sem, w_used.upto(L, g))
                else:
                    eng.wait_ge(y_done.sem, y_done.upto(L, (0 if s == 1 else 5) + n + 1))
            elif t == 0:
                eng.wait_ge(y_done.sem, y_done.upto(L, 3 + h + 1))
            else:
                eng.wait_ge(w_used.sem, w_used.upto(L, MIX0 + M_WO + 2 * h + 2))

        def tr_view(bank):
            return psum[:, bank, :].rearrange("p (k n) -> p k n", k=4)

        def hid_cols(j):
            return slice(KCH * S, 2 * KCH * S) if isinstance(j, int) and j == NCH - 1 else slice(0, KCH * S)

        def gu_group(f, j):
            return f * FFN2_0 + (1 if isinstance(j, int) and j == 0 else 3 * j)

        def part_products(eng, L, p, part):
            products(eng, L, part_done, 2 * p + part // 2, part % 2, MIX0 + M_PAIR + 2 * p + part // 2)

        def banks(b):
            return psum[:, b:b + 2, :].rearrange("p b n -> p (b n)")

        def mix_source(m, L):
            def rows(w, a, k, c0, n):
                return w[L, a * P:(a + k) * P, c0:c0 + n].rearrange("(k p) n -> p k n", p=P)
            if m < M_KV:
                return rows(w_in, 4 * (m - M_Q), 4, C_Q, QR)
            if m < M_POOL:
                return rows(w_in, 4 * (m - M_KV), 4, C_KV, KVW)
            if m < M_G0:
                return rows(w_in, 4 * (m - M_POOL), 4, C_POOL, POOL)
            for c, m0 in enumerate((M_G0, M_G1, M_G2, M_G3)):
                if m0 <= m < m0 + 2:
                    return rows(w_in, 4 * (m - m0), 4, C_GATE + c * N512, N512)
            if m == M_MAPS:
                return pool_maps[L].rearrange("g c d -> c g d")
            if m < M_PP:
                p, kv = (m - M_PAIR) // 2, (m - M_PAIR) % 2
                return rows(w_ukv, 0, 2, p * N512, N512) if kv else rows(w_uq, 0, 3, p * 2 * QK, 2 * QK)
            if m < M_AP:
                return rows(w_pool_proj, 0, 4, (m - M_PP) * N512, N512)
            if m < M_WO:
                i = m - M_AP
                return rows(w_attn_proj, 4 * (i // 2), 4, (i % 2) * N512, N512)
            i = m - M_WO
            return rows(w_out, 4 * (i % 2), 4, (i // 2) * N512, N512)

        def split_pieces(m):
            if m is None or m < M_PAIR or m >= M_PP or (m - M_PAIR) % 2:
                n = GROUP
                if m is not None:
                    k, w = {M_Q: (4, QR), M_KV: (4, KVW), M_MAPS: (PG, P)}.get(m if m != 1 and m != 3 else m - 1, (4, N512))
                    if M_PAIR <= m < M_PP:
                        k = 2
                    n = k * w
                return [(lambda s: s[:, 0:n], lambda s: s[:, 0:n])]
            def dst(a, b):
                return lambda s: s[:, 0:3 * N512].rearrange("p (k h n) -> p k h n", k=3, n=P)[:, :, 2:4, a:b]
            def src(a, b):
                return lambda s: s[:, 0:6 * QK].rearrange("p (k h n) -> p k h n", k=3, h=2)[:, :, :, a:b]
            h = ROPE // 2
            return [(lambda s: s[:, 0:3 * N512].rearrange("p (k h n) -> p k h n", k=3, n=P)[:, :, 0:2, :], src(0, NOPE)),
                    (dst(0, 2 * h), src(NOPE, QK)),
                    (dst(2 * h, 3 * h), src(NOPE + h, QK)),
                    (dst(3 * h, 4 * h), src(NOPE, NOPE + h))]

        block = ctx.enter_context(nc.Block())

        @block.sync
        def _(sp):
            def load(L, q, r, src, dst=None):
                if dst is None:
                    k, n = src.shape[1:]
                    dst = raw[:, r, 0:k * n].rearrange("p (k n) -> p k n", k=k)
                sp.wait_ge(w_lo_done.sem, w_lo_done.upto(L, RING * q + r + 1 - RING))
                sp.sem_inc(loads_begun, 1)
                sp.dma_start(dst, src).then_inc(raw_landed[r], 16)

            def load_up(L, f, q, r, j, a):
                src = ups[f][L, a * 4 * P:(a + 1) * 4 * P, :].rearrange("(k p) (u n) -> p k u n", p=P, u=2)
                dst = raw[:, r, :].rearrange("p (k u n) -> p k u n", k=4, u=2)
                load(L, q, r, src[:, :, 0, bass.ds(j * CH, CH)], dst[:, :, 0, :])
                sp.dma_start(dst[:, :, 1, :], src[:, :, 1, bass.ds(j * CH, CH)]).then_inc(raw_landed[r], 16)

            def load_down(L, f, q, r, j):
                load(L, q, r, downs[f][L, bass.ds(j * CH, CH), :].rearrange("(k p) n -> p k n", p=P))

            def ffn(L, f):
                q0 = f * FFN2_0 // RING
                load_up(L, f, q0, 0, 0, 0)
                load_up(L, f, q0, 1, 0, 1)
                with nc.sync.Fori(1, NCH) as j:
                    load_up(L, f, q0 + j - 1, 2, j, 0)
                    load_up(L, f, q0 + j, 0, j, 1)
                    load_down(L, f, q0 + j, 1, j - 1)
                load_down(L, f, q0 + NCH - 1, 2, NCH - 1)

            with nc.sync.Fori(0, DEPTH) as L:
                ffn(L, 0)
                for m in range(MIX_GROUPS):
                    load(L, (MIX0 + m) // RING, m % RING, mix_source(m, L))
                ffn(L, 1)

            out_v = out.rearrange("b (t p) d -> p (b t) d", p=P)
            for t in range(TB):
                sp.wait_ge(out_rows, t + 1)
                sp.dma_start(out_v[:, t], xs[:, t, :]).then_inc(out_landed, 16)
            sp.wait_ge(out_landed, 16 * TB)

        @block.gpsimd
        def _(pool):
            def broadcast(dst, src, landed):
                return pool.dma_start(dst, src.to_broadcast(list(dst.shape))).then_inc(landed, 16)

            pool.memset(half_neg[:, :], -0.5).then_inc(exponent_set, 1)
            pool.memset(neg_one[:, :], -1.0).then_inc(exponent_set, 1)

            def load_tables():
                pool.wait_ge(raw_landed[1], 32)
                pool.dma_start(rotary, c_rotary).then_inc(pos_landed, 16)
                pool.dma_start(pos_row_i, positions[0:1, :].to_broadcast([P, S])).then_inc(pos_landed, 16)
                with nc.allow_non_contiguous_dma(reason="256 positions"):
                    pool.dma_start(pos_col_i[:, :], positions.rearrange("b (t p) -> p (b t)", p=P)).then_inc(pos_landed, 16)
                pool.dma_start(causal_f, c_causal).then_inc(const_landed, 16)
                pool.dma_start(window_f, c_window).then_inc(const_landed, 16)
                broadcast(inv_count[:, :], c_inv_count, const_landed)
                with nc.allow_non_contiguous_dma(reason="1024 scales"):
                    pool.dma_start(pscale[:, :, :], pool_scale.rearrange("l (g p) -> p l g", p=P)).then_inc(const_landed, 16)

            def rsqrt(dst, src, width, done):
                return pool.tensor_tensor(dst, src, half_neg[:, 0:width], ALU.pow).then_inc(done.sem, 1)

            def norm_rsqrt(L, s):
                for t in range(TB):
                    pool.wait_ge(ms_done.sem, ms_done.upto(L, TB * s + t + 1))
                    rsqrt(stat[:, NRS + t:NRS + t + 1], stat[:, NMS + t:NMS + t + 1], 1, rstd_done)

            step = [0]

            def rot_op(ins):
                step[0] += 1
                ins.then_inc(rot_step, 1)
                pool.wait_ge(rot_step, step[0])

            def scalar(dst, a, c0, op0, c1=None, op1=None):
                if op1 is None:
                    rot_op(pool.tensor_scalar(dst, a, c0, None, op0))
                else:
                    rot_op(pool.tensor_scalar(dst, a, c0, c1, op0, op1))

            def tensor(dst, a, b, op):
                rot_op(pool.tensor_tensor(dst, a, b, op))

            def rotary_angles():
                pool.wait_ge(pos_landed, 16 * 3)
                rot_op(pool.tensor_copy(pos_row, pos_row_i))
                rot_op(pool.tensor_copy(pos_col[:, :], pos_col_i[:, :]))
                tensor(angle[:, 0:S], pos_row, freq[:, 0:S], ALU.mult)
                for t in range(TB):
                    cols = slice(S + t * P, S + (t + 1) * P)
                    tensor(angle[:, cols], freq[:, cols], pos_col[:, t:t + 1].to_broadcast([P, P]), ALU.mult)
                pool.wait_ge(const_landed, 16 * 4)
                pool.wait_ge(ident_landed, 16)
                rot_op(pool.tensor_copy(ident_r[:, :], ident[:, :]))
                rot_op(pool.tensor_copy(causal_r[:, :], causal_f))
                for unit in (1024.0, 1.0):
                    scalar(turns, angle[:, :], 1.0 / (2 * np.pi * unit), ALU.mult, ROUND, ALU.add)
                    scalar(turns, turns, -ROUND, ALU.add)
                    for c in TWO_PI:
                        scalar(product, turns, -c * unit, ALU.mult)
                        tensor(angle[:, :], product, angle[:, :], ALU.add)
                tensor(angle[:, :], angle[:, :], phase, ALU.add)
                scalar(turns, angle[:, :], PI_LOW, ALU.is_gt, -2 * np.pi, ALU.mult)
                tensor(angle[:, :], angle[:, :], turns, ALU.add)
                scalar(angle[:, :], angle[:, :], PI_LOW, ALU.min, -PI_LOW, ALU.max)
                tensor(angle[:, :], angle[:, :], sign, ALU.mult)
                rot_op(pool.tensor_copy(window[:, :], window_f))

            def normalise(L, p):
                row, st = scores[:, p % 2, :], stat2[:, p % 2, :]
                pool.wait_ge(exp_done.sem, exp_done.upto(L, p + 1))
                pool.tensor_tensor(st[:, 12:16], st[:, 8:12], neg_one[:, :], ALU.pow).then_inc(inv_done.sem, 1)
                pool.wait_ge(inv_done.sem, inv_done.upto(L, p + 1))
                for cols, i, n in ((slice(0, 2 * S), 12, S), (slice(2 * S, 3 * S), 14, P)):
                    v = row[:, cols].rearrange("p (h n) -> p h n", h=2)
                    last = pool.tensor_tensor(v, v, st[:, i:i + 2].unsqueeze(2).to_broadcast([P, 2, n]), ALU.mult)
                last.then_inc(prob_done.sem, 1)

            def gained(h, t):
                pool.tensor_tensor(xs[:, t, half(h)], x[:, t, half(h)], gain[:, half(h)],
                                   ALU.mult).then_inc(normed[h].sem, 1)

            def second_half(L, s):
                pool.wait_ge(gain_landed, (L * 3 + s) * 16)
                for t in range(TB):
                    pool.wait_ge(x_ready.sem, x_ready.upto(L, quarter(s, 1, t)))
                    gained(1, t)

            def next_gain(L, s):
                for h in range(2):
                    pool.wait_ge(normed[h].sem, normed[h].upto(L, normed_count(s, TB - 1)))
                broadcast(gain[:, :], gains[bass.ds(L * 3 + s + 1, 1), :], gain_landed)

            def rest(L):
                broadcast(lat_gain[:, 0:QR], q_latent_norm[bass.ds(L, 1), :], latg_landed)
                broadcast(lat_gain[:, QR:QR + KVR], kv_latent_norm[bass.ds(L, 1), :], latg_landed)
                for t in range(TB):
                    broadcast(gates[:, t, :], b_gate[bass.ds(L, 1), :], bias_landed)
                next_gain(L, 0)
                second_half(L, 1)
                next_gain(L, 1)
                norm_rsqrt(L, 1)
                for i in range(2):
                    pool.wait_ge(lat_ms.sem, lat_ms.upto(L, i + 1))
                    rs = stat[:, LRS + 2 * i:LRS + 2 * i + 2]
                    rsqrt(rs, stat[:, LMS + 2 * i:LMS + 2 * i + 2], 2, lat_rstd)
                    pool.wait_ge(lat_rstd.sem, lat_rstd.upto(L, i + 1))
                    pool.tensor_tensor(rs, rs, stat[:, NRS:NRS + TB], ALU.mult).then_inc(lat_scale.sem, 1)
                for p in range(PAIRS):
                    normalise(L, p)
                second_half(L, 2)
                next_gain(L, 2)
                norm_rsqrt(L, 2)
                second_half(L, 3)

            pool.wait_ge(exponent_set, 2)
            pool.wait_ge(gain0_landed, 16)
            for t in range(TB):
                pool.wait_ge(x_landed[t], 16)
                gained(0, t)
            pool.sem_inc(x_ready.sem, QUARTERS)
            for t in range(TB):
                gained(1, t)
            load_tables()
            norm_rsqrt(0, 0)
            rotary_angles()
            assert step[0] == ROT_STEPS, step[0]
            with nc.gpsimd.Fori(0, DEPTH) as L:
                rest(L)
                norm_rsqrt(L, 3)

        @block.scalar
        def _(act):
            def split(L, q, r, m=None, twos=0):
                per_layer = GROUPS // RING + 2 * UPS[r]
                act.wait_ge(raw_landed[r], (L * per_layer + q + 1 + twos) * 16)
                act.wait_ge(w_used.sem, w_used.upto(L, RING * q + r + 1 - RING))
                for dst, src in split_pieces(m):
                    last = act.activation(dst(w_hi[:, r, :]), src(raw[:, r, :]), ACT.Copy)
                last.then_inc(w_hi_done.sem, 1)

            def split_mix(L, m):
                if m < MIX_GROUPS:
                    split(L, (MIX0 + m) // RING, m % RING, m, UPS[m % RING])
                else:
                    r = m - MIX_GROUPS
                    split(L, FFN2_0 // RING, r, None, UPS[r] + 1)

            def high(L, after, n, dst, src, done):
                act.wait_ge(after.sem, after.upto(L, n))
                act.activation(dst, src, ACT.Copy).then_inc(done.sem, 1)

            def squares(L, s):
                for t in range(TB):
                    act.wait_ge(x_ready.sem, x_ready.upto(L, quarter(s, 1, t)))
                    if t:
                        act.wait_ge(sq_done.sem, sq_done.upto(L, TB * s + t))
                    act.activation(square_junk, x[:, t, :], ACT.Square,
                                   accum_out=stat[:, NSQ + t:NSQ + t + 1]).then_inc(sq_done.sem, 1)

            def norm(L, s, h):
                for t in range(TB):
                    high(L, norm_tr, quarter(s, h, t), xT[:, 0, 4 * h:4 * h + 4, blk(t)],
                         tr_view(NORM_T_BANK[h][t]), norm_hi)

            def rstd(t):
                return stat[:, NRS + t:NRS + t + 1]

            def silu(L, f, j):
                if isinstance(j, int) and j == 0:
                    act.wait_ge(rstd_done.sem, rstd_done.upto(L, 2 * TB * f + TB))
                for t in range(TB):
                    products(act, L, gu_done, f * NCH + j, t, gu_group(f, j))
                    act.activation(silu_sb[:, t, :], psum[:, GU_BANK + t, 0:CH], ACT.Silu,
                                   scale=rstd(t)).then_inc(silu_done.sem, 1)

            def hidden(L, f, j):
                high(L, hid_tr, f * NCH + j + 1, small_T[:, 0, hid_cols(j)], psum[:, TR_BANK, :], hid_hi)

            def ffn(L, f):
                q0 = f * FFN2_0 // RING
                u0, u2 = f * UPS[0], f * UPS[2]
                silu(L, f, 0)
                split(L, q0 + 1, 0, None, u0 + 2)
                with nc.scalar.Fori(1, NCH - 1) as j:
                    split(L, q0 + j, 1, None, (f + 1) * UPS[1])
                    hidden(L, f, j - 1)
                    split(L, q0 + j, 2, None, u2 + j + 1)
                    silu(L, f, j)
                    split(L, q0 + j + 1, 0, None, u0 + j + 2)
                j = NCH - 1
                split(L, q0 + j, 1, None, (f + 1) * UPS[1])
                hidden(L, f, j - 1)
                split(L, q0 + j, 2, None, u2 + UPS[2])
                silu(L, f, j)
                if f == 0:
                    split_mix(L, 0)
                hidden(L, f, j)

            def operands(L, p, which):
                for part in which:
                    src = psum[:, 2 + part, :]
                    if part == QRO:
                        high(L, rope_done, p + 1, flat(pair(p, part), 0), src, part_hi)
                        continue
                    if part == VV and p >= 2:
                        act.wait_ge(pv_done.sem, pv_done.upto(L, p - 1))
                    part_products(act, L, p, part)
                    act.activation(flat(pair(p, part), 0), src, ACT.Copy).then_inc(part_hi.sem, 1)

            def softmax(L, p):
                row = scores[:, p % 2, :]
                st = stat2[:, p % 2, :]
                act.wait_ge(bias_done.sem, bias_done.upto(L, p + 1))
                for i, (cols, bank) in enumerate(zip(ROWS, (6, 6, 7, 7))):
                    n = cols.stop - cols.start
                    src = psum[:, bank, (i % 2) * n:(i % 2 + 1) * n]
                    last = act.activation(row[:, cols], src, ACT.Exp, scale=SCALE,
                                          bias=st[:, 4 + i:5 + i], accum_out=st[:, 8 + i:9 + i])
                last.then_inc(exp_done.sem, 1)

            def probs(L, p):
                high(L, prob_tr, p + 1, small_T[:, 0, 0:3 * S], banks(0)[:, 0:3 * S], prob_hi)

            def heads_out(L, p):
                high(L, pv_done, p + 1, flat(oT[:, :, 2 * p:2 * p + 2, :], 0), psum[:, 0, :], o_hi)

            def gate(L, c):
                for t in range(TB):
                    g = gates[:, t, c * N512:(c + 1) * N512]
                    act.wait_ge(gate_biased.sem, gate_biased.upto(L, TB * c + t + 1))
                    act.activation(g, g, ACT.Sigmoid).then_inc(gate_sig.sem, 1)

            def latent_squares(L, i):
                done, m, bank, dst, n = ((q_done, M_Q, 4, qlat_s, QR), (kv_done, M_KV, 2, kvlat_s, KVR))[i]
                for t in range(TB):
                    products(act, L, done, 0, t, MIX0 + m + 1)
                    act.wait_ge(rstd_done.sem, rstd_done.upto(L, TB + t + 1))
                    c = LSQ + 2 * i + t
                    act.activation(dst[:, t, 0:n], psum[:, bank + t, 0:n], ACT.Square, scale=rstd(t),
                                   accum_out=stat[:, c:c + 1]).then_inc(lat_sq.sem, 1)

            def latent(L, i):
                for t in range(TB):
                    high(L, lat_tr, 2 * i + t + 1, latT[:, 0, 3 * i:3 * i + 3, blk(t)],
                         psum[:, (4, 2)[i] + t, 0:3 * P].rearrange("p (k n) -> p k n", k=3), lat_hi)

            def mixer(L):
                split_mix(L, 3)
                latent_squares(L, 0)
                split_mix(L, 4)
                split_mix(L, 5)
                latent_squares(L, 1)
                split_mix(L, 6)
                split_mix(L, 7)
                for t in range(TB):
                    products(act, L, xp_done, 0, t, MIX0 + M_POOL + 1)
                    act.activation(xpt[:, 0, t, :], psum[:, 6 + t, :], ACT.Copy, scale=rstd(t)).then_inc(xp_hi.sem, 1)
                split_mix(L, 8)
                act.wait_ge(rot_step, ROT_STEPS)
                act.activation(rot[:, :], angle[:, :], ACT.Sin).then_inc(rotary_ready.sem, 1)
                split_mix(L, 9)
                gate(L, 0)
                latent(L, 0)
                split_mix(L, 10)
                split_mix(L, 11)
                gate(L, 1)
                latent(L, 1)
                high(L, pool_scaled, 1, flat(poolT, 0), tmp, pool_hi)
                split_mix(L, 12)
                split_mix(L, 13)
                gate(L, 2)
                split_mix(L, 14)
                high(L, pool_scaled, 2, flat(mixT, 0), tmp, pool_hi)
                split_mix(L, 15)
                split_mix(L, 16)
                split_mix(L, 17)
                gate(L, 3)
                operands(L, 0, (QN,))
                act.activation(table_junk[:, :], half_neg[:, 0:1], ACT.Exp)
                operands(L, 0, (QRO,))
                split_mix(L, 18)
                operands(L, 0, (KN, VV))
                split_mix(L, 19)
                operands(L, 1, (QN, QRO))
                split_mix(L, 20)
                operands(L, 1, (KN, VV))
                split_mix(L, 21)
                softmax(L, 0)
                operands(L, 2, (QN, ))
                split_mix(L, 22)
                operands(L, 2, (QRO, KN))
                probs(L, 0)
                split_mix(L, 23)
                softmax(L, 1)
                operands(L, 3, (QN, QRO))
                operands(L, 2, (VV,))
                heads_out(L, 0)
                operands(L, 3, (KN,))
                split_mix(L, 24)
                probs(L, 1)
                split_mix(L, 25)
                softmax(L, 2)
                operands(L, 3, (VV,))
                heads_out(L, 1)
                probs(L, 2)
                split_mix(L, 26)
                softmax(L, 3)
                heads_out(L, 2)
                probs(L, 3)
                split_mix(L, 27)
                heads_out(L, 3)
                split_mix(L, 28)
                split_mix(L, 29)
                split_mix(L, 30)
                merge_norm(L, 0)
                split_mix(L, 31)
                merge_norm(L, 1)
                split_mix(L, 32)
                split_mix(L, 33)
                split_mix(L, 34)
                norm(L, 2, 0)

            def merge_norm(L, h):
                for t in range(TB):
                    high(L, mrg_tr, TB * h + t + 1, xT[:, 0, 4 * h:4 * h + 4, blk(t)],
                         tr_view(MERGE_T_BANK[h][t]), mrg_hi)

            act.dma_start(ident[:, :], c_ident).then_inc(ident_landed, 16)
            act.dma_start(x[:, 0, :], x_in[0, blk(0), :]).then_inc(x_landed[0], 16)
            act.dma_start(gain[:, :], gains[0:1, :].to_broadcast([P, D])).then_inc(gain0_landed, 16)
            act.dma_start(x[:, 1, :], x_in[0, blk(1), :]).then_inc(x_landed[1], 16)
            act.wait_ge(exponent_set, 1)
            act.activation(table_junk[:, :], half_neg[:, 0:1], ACT.Silu)
            with nc.scalar.Fori(0, DEPTH) as L:
                split(L, 0, 0, None, 1)
                norm(L, 0, 0)
                split(L, 0, 1, None, 1)
                squares(L, 0)
                norm(L, 0, 1)
                split(L, 0, 2, None, 1)
                ffn(L, 0)
                split_mix(L, 1)
                norm(L, 1, 0)
                split_mix(L, 2)
                norm(L, 1, 1)
                squares(L, 1)
                mixer(L)
                split(L, FFN2_0 // RING, 2, None, UPS[2] + 1)
                norm(L, 2, 1)
                squares(L, 2)
                act.activation(table_junk[:, :], half_neg[:, 0:1], ACT.Silu)
                ffn(L, 1)
            squares(DEPTH, 0)

        @block.vector
        def _(dve):
            def mul_add(dst, a, c, b):
                return dve.scalar_tensor_tensor(out=dst, in0=a, scalar=c, in1=b, op0=ALU.mult, op1=ALU.add)

            def times(dst, a, b):
                return dve.tensor_tensor(dst, a, b, ALU.mult)

            def minus(dst, a, b):
                return dve.tensor_tensor(dst, a, b, ALU.subtract)

            def split(L, q, r, m=None):
                dve.wait_ge(w_hi_done.sem, w_hi_done.upto(L, RING * q + r + 1))
                for dst, src in split_pieces(m):
                    last = minus(dst(w_lo[:, r, :]), src(raw[:, r, :]), dst(w_hi[:, r, :].bitcast(F32)))
                last.then_inc(w_lo_done.sem, 1)

            def split_mix(L, m):
                if m < MIX_GROUPS:
                    split(L, (MIX0 + m) // RING, m % RING, m)
                else:
                    split(L, FFN2_0 // RING, m - MIX_GROUPS)

            def low(L, high_done, n, dst, src, hi, done):
                dve.wait_ge(high_done.sem, high_done.upto(L, n))
                minus(dst, src, hi.bitcast(F32)).then_inc(done.sem, 1)

            def update(L, s, h, t):
                y_ready(dve, L, s, h, t)
                bank = 2 * t + h
                mul_add(x[:, t, half(h)], psum[:, bank, :], 1.0 if s == 2 else 0.5,
                        x[:, t, half(h)]).then_inc(x_ready.sem, 1)
                if h == 0:
                    dve.wait_ge(x_ready.sem, x_ready.upto(L, quarter(s, h, t)))
                    gained(t)

            def gained(t):
                times(xs[:, t, half(0)], x[:, t, half(0)], gain[:, half(0)]).then_inc(normed[0].sem, 1)

            def mean_squares(L, s):
                for t in range(TB):
                    dve.wait_ge(sq_done.sem, sq_done.upto(L, TB * s + t + 1))
                    dve.tensor_scalar(stat[:, NMS + t:NMS + t + 1], stat[:, NSQ + t:NSQ + t + 1], 1.0 / D, EPS,
                                      ALU.mult, ALU.add).then_inc(ms_done.sem, 1)

            def norm_low(L, s, h, t):
                low(L, norm_hi, quarter(s, h, t), xT[:, 1, 4 * h:4 * h + 4, blk(t)],
                    tr_view(NORM_T_BANK[h][t]), xT[:, 0, 4 * h:4 * h + 4, blk(t)], norm_lo)

            def rstd(t):
                return stat[:, NRS + t:NRS + t + 1]

            def into_mixer(L):
                dve.wait_ge(gain_landed, (L * 3 + 1) * 16)
                update(L, 1, 0, 0)
                update(L, 1, 0, 1)
                norm_low(L, 1, 0, 0)
                update(L, 1, 1, 0)
                norm_low(L, 1, 0, 1)
                update(L, 1, 1, 1)
                split_mix(L, 1)
                norm_low(L, 1, 1, 0)
                norm_low(L, 1, 1, 1)
                split_mix(L, 2)
                mean_squares(L, 1)

            def into_ffn2(L):
                dve.wait_ge(gain_landed, (L * 3 + 2) * 16)
                update(L, 2, 0, 0)
                update(L, 2, 0, 1)
                split_mix(L, 33)
                split_mix(L, 34)
                norm_low(L, 2, 0, 0)
                update(L, 2, 1, 0)
                norm_low(L, 2, 0, 1)
                update(L, 2, 1, 1)
                norm_low(L, 2, 1, 0)
                split(L, FFN2_0 // RING, 2)
                norm_low(L, 2, 1, 1)
                mean_squares(L, 2)

            def hidden_product(L, f, j):
                for t in range(TB):
                    n = (f * NCH + j) * TB + t + 1
                    dve.wait_ge(silu_done.sem, silu_done.upto(L, n))
                    dve.scalar_tensor_tensor(out=act_sb[:, t, :], in0=psum[:, GU_BANK + t, CH:2 * CH], scalar=rstd(t),
                                             in1=silu_sb[:, t, :], op0=ALU.mult, op1=ALU.mult).then_inc(act_done.sem, 1)

            def hidden(L, f, j):
                low(L, hid_hi, f * NCH + j + 1, small_T[:, 1, hid_cols(j)], psum[:, TR_BANK, :],
                    small_T[:, 0, hid_cols(j)], hid_lo)

            def ffn(L, f):
                q0 = f * FFN2_0 // RING
                hidden_product(L, f, 0)
                split(L, q0 + 1, 0)
                with nc.vector.Fori(1, NCH - 1) as j:
                    split(L, q0 + j, 1)
                    hidden(L, f, j - 1)
                    split(L, q0 + j, 2)
                    hidden_product(L, f, j)
                    split(L, q0 + j + 1, 0)
                j = NCH - 1
                split(L, q0 + j, 1)
                hidden(L, f, j - 1)
                split(L, q0 + j, 2)
                hidden_product(L, f, j)
                if f == 0:
                    split_mix(L, 0)
                hidden(L, f, j)

            def gate(L, c):
                for t in range(TB):
                    g = gates[:, t, c * N512:(c + 1) * N512]
                    dve.wait_ge(bias_landed, (L + 1) * 16 * TB)
                    products(dve, L, gate_done, c, t, MIX0 + (M_G0, M_G1, M_G2, M_G3)[c] + 1)
                    mul_add(g, psum[:, t, :], rstd(t), g).then_inc(gate_biased.sem, 1)

            def latent_norm(L, i):
                bank, dst, n, g0 = ((4, qlat_s, QR, 0), (2, kvlat_s, KVR, QR))[i]
                dve.wait_ge(lat_scale.sem, lat_scale.upto(L, i + 1))
                dve.wait_ge(latg_landed, (L + 1) * 32)
                for t in range(TB):
                    c = LRS + 2 * i + t
                    last = dve.scalar_tensor_tensor(out=dst[:, t, 0:n], in0=psum[:, bank + t, 0:n],
                                                    scalar=stat[:, c:c + 1], in1=lat_gain[:, g0:g0 + n],
                                                    op0=ALU.mult, op1=ALU.mult)
                last.then_inc(lat_normed.sem, 1)

            def latent_mean_squares(L, i):
                n = (QR, KVR)[i]
                dve.wait_ge(lat_sq.sem, lat_sq.upto(L, 2 * i + 2))
                dve.tensor_scalar(stat[:, LMS + 2 * i:LMS + 2 * i + 2], stat[:, LSQ + 2 * i:LSQ + 2 * i + 2],
                                  1.0 / n, EPS, ALU.mult, ALU.add).then_inc(lat_ms.sem, 1)

            def rotate_key(L):
                h = ROPE // 2
                k = kvlat_s[:, :, KVR:KVR + ROPE]
                for t in range(TB):
                    last = dve.tensor_scalar(k[:, t, :], psum[:, 2 + t, KVR:KVR + ROPE], rstd(t), None, ALU.mult)
                last.then_inc(krot_step.sem, 1)
                dve.wait_ge(krot_step.sem, krot_step.upto(L, 1))
                dve.wait_ge(rotary_ready.sem, rotary_ready.upto(L, 1))
                times(rot_a, k, rot_t[:, :, 0, :])
                times(rot_b[:, :, 0:h], k[:, :, h:], rot_t[:, :, 1, 0:h])
                times(rot_b[:, :, h:], k[:, :, 0:h], rot_t[:, :, 1, h:]).then_inc(krot_step.sem, 1)
                dve.wait_ge(krot_step.sem, krot_step.upto(L, 2))
                for i in range(2):
                    dve.tensor_tensor(kvlat_s[:, :, KVR + i * ROPE:KVR + (i + 1) * ROPE], rot_a, rot_b,
                                      ALU.add).then_inc(krot_step.sem, 1)

            def latent(L, i):
                for t in range(TB):
                    low(L, lat_hi, 2 * i + t + 1, latT[:, 1, 3 * i:3 * i + 3, blk(t)],
                        psum[:, (4, 2)[i] + t, 0:3 * P].rearrange("p (k n) -> p k n", k=3),
                        latT[:, 0, 3 * i:3 * i + 3, blk(t)], lat_lo)

            def pool_scale_rows(L, i):
                products(dve, L, pool_done, 0, i, MIX0 + M_MAPS)
                src = banks(6)
                if i == 0:
                    sums, means = (v.rearrange("p (g n) -> p g n", g=PG) for v in (src, tmp))
                    times(means[:, :, 0:RAMP], sums[:, :, 0:RAMP], inv_count[:, :, :])
                    last = times(means[:, :, RAMP:], sums[:, :, RAMP:],
                                 inv_count[:, :, RAMP - 1:RAMP].to_broadcast([P, PG, S - RAMP]))
                else:
                    scale = pscale[:, bass.ds(L, 1), :].rearrange("p l g -> p (l g)")
                    last = dve.tensor_tensor(tmp.rearrange("p (g n) -> p g n", g=PG),
                                             src.rearrange("p (g n) -> p g n", g=PG),
                                             scale.unsqueeze(2).to_broadcast([P, PG, S]), ALU.mult)
                last.then_inc(pool_scaled.sem, 1)

            def pool_low(L, i):
                dst = (poolT, mixT)[i]
                low(L, pool_hi, i + 1, flat(dst, 1), tmp, flat(dst, 0), pool_lo)

            def operands(L, p, which):
                for part in which:
                    src = psum[:, 2 + part, :]
                    if part == QRO:
                        part_products(dve, L, p, part)
                        both = src.rearrange("p (h n) -> p h n", h=2)
                        times(both, both, rot_f.unsqueeze(1).to_broadcast([P, 2, S])).then_inc(rope_done.sem, 1)
                    low(L, part_hi, part_count(p, part), flat(pair(p, part), 1), src, flat(pair(p, part), 0), part_lo)

            def maxima(L, p):
                st = stat2[:, p % 2, :]
                two = lambda v: v.rearrange("p (h n) -> p h n", h=2)
                dve.wait_ge(score_done.sem, score_done.upto(L, p + 1))
                dve.tensor_reduce(st[:, 0:2], two(psum[:, 6, :]), AX.X, ALU.max)
                dve.tensor_reduce(st[:, 2:4], two(psum[:, 7, 0:S]), AX.X, ALU.max).then_inc(max_done.sem, 1)
                dve.wait_ge(max_done.sem, max_done.upto(L, p + 1))
                dve.tensor_scalar(st[:, 4:8], st[:, 0:4], -SCALE, None, ALU.mult).then_inc(bias_done.sem, 1)

            def probs(L, p):
                low(L, prob_hi, p + 1, small_T[:, 1, 0:3 * S], banks(0)[:, 0:3 * S], small_T[:, 0, 0:3 * S], prob_lo)

            def heads_out(L, p):
                o = oT[:, :, 2 * p:2 * p + 2, :]
                low(L, o_hi, p + 1, flat(o, 1), psum[:, 0, :], flat(o, 0), o_lo)

            def gate_a(L, n):
                for t in range(TB):
                    g = gates[:, t, n * N512:(n + 1) * N512]
                    products(dve, L, a_done, n, t, MIX0 + M_PP + n)
                    times(g, g, psum[:, 2 + 2 * n + t, :]).then_inc(a_gated.sem, 1)

            def gate_b(L, n):
                for t in range(TB):
                    cols = slice(n * N512, (n + 1) * N512)
                    products(dve, L, b_done, n, t, MIX0 + M_AP + 2 + n)
                    times(xs[:, t, cols], gates[:, t, D + n * N512:D + (n + 1) * N512],
                          psum[:, 2 + 2 * n + t, :]).then_inc(b_gated.sem, 1)
                    dve.wait_ge(b_gated.sem, b_gated.upto(L, TB * n + t + 1))
                    dve.tensor_tensor(xs[:, t, cols], xs[:, t, cols], gates[:, t, cols], ALU.add).then_inc(merged.sem, 1)

            def merge_low(L, h, t):
                low(L, mrg_hi, TB * h + t + 1, xT[:, 1, 4 * h:4 * h + 4, blk(t)],
                    tr_view(MERGE_T_BANK[h][t]), xT[:, 0, 4 * h:4 * h + 4, blk(t)], mrg_lo)

            def mixer(L):
                split_mix(L, 3)
                dve.wait_ge(rstd_done.sem, rstd_done.upto(L, 2 * TB))
                latent_mean_squares(L, 0)
                split_mix(L, 4)
                latent_norm(L, 0)
                split_mix(L, 5)
                latent_mean_squares(L, 1)
                split_mix(L, 6)
                latent_norm(L, 1)
                split_mix(L, 7)
                for t in range(TB):
                    dve.wait_ge(xp_hi.sem, xp_hi.upto(L, t + 1))
                    dve.scalar_tensor_tensor(out=xpt[:, 1, t, :], in0=psum[:, 6 + t, :], scalar=rstd(t),
                                             in1=xpt[:, 0, t, :].bitcast(F32), op0=ALU.mult,
                                             op1=ALU.subtract).then_inc(xp_lo.sem, 1)
                split_mix(L, 8)
                split_mix(L, 9)
                gate(L, 0)
                latent(L, 0)
                rotate_key(L)
                split_mix(L, 10)
                split_mix(L, 11)
                gate(L, 1)
                latent(L, 1)
                pool_scale_rows(L, 0)
                pool_low(L, 0)
                split_mix(L, 12)
                split_mix(L, 13)
                gate(L, 2)
                split_mix(L, 14)
                pool_scale_rows(L, 1)
                pool_low(L, 1)
                split_mix(L, 15)
                split_mix(L, 16)
                gate(L, 3)
                split_mix(L, 17)
                operands(L, 0, (QN, QRO))
                split_mix(L, 18)
                operands(L, 0, (KN, VV))
                split_mix(L, 19)
                operands(L, 1, (QN, QRO))
                split_mix(L, 20)
                maxima(L, 0)
                operands(L, 1, (KN, VV))
                split_mix(L, 21)
                operands(L, 2, (QN,))
                split_mix(L, 22)
                operands(L, 2, (QRO, KN))
                probs(L, 0)
                maxima(L, 1)
                split_mix(L, 23)
                operands(L, 3, (QN, QRO))
                operands(L, 2, (VV,))
                heads_out(L, 0)
                operands(L, 3, (KN,))
                split_mix(L, 24)
                probs(L, 1)
                maxima(L, 2)
                split_mix(L, 25)
                operands(L, 3, (VV,))
                heads_out(L, 1)
                dve.wait_ge(gate_sig.sem, gate_sig.upto(L, 4 * TB))
                gate_a(L, 0)
                probs(L, 2)
                maxima(L, 3)
                split_mix(L, 26)
                heads_out(L, 2)
                probs(L, 3)
                gate_a(L, 1)
                split_mix(L, 27)
                heads_out(L, 3)
                split_mix(L, 28)
                split_mix(L, 29)
                gate_b(L, 0)
                split_mix(L, 30)
                merge_low(L, 0, 0)
                merge_low(L, 0, 1)
                gate_b(L, 1)
                merge_low(L, 1, 0)
                split_mix(L, 31)
                merge_low(L, 1, 1)
                split_mix(L, 32)

            dve.sem_inc(w_lo_done.sem, 1)
            dve.wait_ge(x_landed[0], 16)
            dve.sem_inc(w_lo_done.sem, RING - 1)
            with nc.vector.Fori(0, DEPTH) as L:
                dve.wait_ge(w_hi_done.sem, w_hi_done.upto(L, 1))
                early, late = slice(0, GROUP // 2), slice(GROUP // 2, GROUP)
                minus(w_lo[:, 0, early], raw[:, 0, early], w_hi[:, 0, early].bitcast(F32)).then_inc(w_lo_half.sem, 1)
                norm_low(L, 0, 0, 0)
                minus(w_lo[:, 0, late], raw[:, 0, late], w_hi[:, 0, late].bitcast(F32)).then_inc(w_lo_done.sem, 1)
                norm_low(L, 0, 0, 1)
                split(L, 0, 1)
                mean_squares(L, 0)
                norm_low(L, 0, 1, 0)
                norm_low(L, 0, 1, 1)
                split(L, 0, 2)
                ffn(L, 0)
                into_mixer(L)
                mixer(L)
                into_ffn2(L)
                ffn(L, 1)
                dve.wait_ge(gain_landed, (L * 3 + 3) * 16)
                for h in range(2):
                    for t in range(TB):
                        update(L, 3, h, t)
            mean_squares(DEPTH, 0)
            dve.wait_ge(normed[1].sem, normed[1].upto(DEPTH, normed_count(0, TB - 1)))
            dve.wait_ge(norm_tr.sem, norm_tr.upto(DEPTH, quarter(0, 0, TB - 1)))
            for t in range(TB):
                dve.wait_ge(rstd_done.sem, rstd_done.upto(DEPTH, t + 1))
                dve.tensor_scalar(xs[:, t, :], xs[:, t, :], rstd(t), None, ALU.mult).then_inc(out_rows, 1)

        @block.tensor
        def _(pe):
            def passes(dst, a_hi, a_lo, b_hi, b_lo, first, last):
                nc.tensor.matmul(dst, a_hi, b_hi, start=first, stop=False)
                nc.tensor.matmul(dst, a_hi, b_lo, start=False, stop=False)
                return nc.tensor.matmul(dst, a_lo, b_hi, start=False, stop=last)

            def wait(ev, L, n):
                pe.wait_ge(ev.sem, ev.upto(L, n))

            def weights(L, q, r):
                wait(w_lo_done, L, RING * q + r + 1)
                return w_hi[:, r, :], w_lo[:, r, :]

            def mix_weights(L, m):
                return weights(L, (MIX0 + m) // RING, m % RING)

            def tiles(dst, src, count, done=None):
                for k in range(count):
                    last = nc.tensor.transpose(dst[:, k * P:(k + 1) * P], src[:, k * P:(k + 1) * P], ident[:, :])
                if done is not None:
                    last.then_inc(done.sem, 1)
                return last

            def turn_norm(L, s, h, t):
                wait(normed[h], L, normed_count(s, t))
                tiles(psum[:, NORM_T_BANK[h][t], :], xs[:, t, half(h)], 4, norm_tr)

            def turn_merged(L, h, t):
                wait(merged, L, TB * h + t + 1)
                tiles(psum[:, MERGE_T_BANK[h][t], :], xs[:, t, half(h)], 4, mrg_tr)

            def project(w, width, bank, a, stat_T, halves, done=None, before=None, halfway=None):
                hi, lo = w
                for t in range(TB):
                    if before is not None:
                        before(t)
                    for k in range(4):
                        if halfway is not None and t == 0 and k == 2:
                            halfway()
                        cols = slice(k * width, (k + 1) * width)
                        last = passes(psum[:, bank[t], 0:width], stat_T[:, 0, 4 * a + k, blk(t)],
                                      stat_T[:, 1, 4 * a + k, blk(t)], hi[:, cols], lo[:, cols],
                                      first=(a == 0 and k == 0), last=(a == halves - 1 and k == 3))
                    if t == 0 and done is not None:
                        last.then_inc(done.sem, 1)
                last.then_inc(w_used.sem, 1)

            def first_product(L, s, w0, w1, width, bank, done, halfway=None):
                def first_half(t):
                    if t == 1:
                        turn_norm(L, s, 1, 0)
                    wait(norm_lo, L, quarter(s, 0, t))

                w = w0()
                project(w, width, bank, 0, xT, 2, before=first_half, halfway=halfway)
                turn_norm(L, s, 1, 1)
                w = w1()
                project(w, width, bank, 1, xT, 2, done, before=lambda t: wait(norm_lo, L, quarter(s, 1, t)))

            def turn_hidden(L, f, j):
                for t in range(TB):
                    wait(act_done, L, (f * NCH + j) * TB + t + 1)
                    for k in range(KCH):
                        last = nc.tensor.transpose(psum[:, TR_BANK, k * S + t * P:k * S + (t + 1) * P],
                                                   act_sb[:, t, k * P:(k + 1) * P], ident[:, :])
                last.then_inc(hid_tr.sem, 1)

            def down(L, f, q, r, j, between=None):
                hi, lo = weights(L, q, r)
                at = hid_cols(j).start
                wait(hid_lo, L, f * NCH + j + 1)
                first, final = isinstance(j, int) and j == 0, isinstance(j, int) and j == NCH - 1
                order = [(t, n) for n in range(2) for t in range(TB)] if final else [(t, n) for t in range(TB) for n in range(2)]
                for i, (t, n) in enumerate(order):
                    if i and between is not None:
                        between(i)
                    for k in range(KCH):
                        cols = slice(k * D + n * N512, k * D + (n + 1) * N512)
                        tile = slice(at + k * S + t * P, at + k * S + (t + 1) * P)
                        last = passes(psum[:, 2 * t + n, :], small_T[:, 0, tile], small_T[:, 1, tile],
                                      hi[:, cols], lo[:, cols], first=(first and k == 0),
                                      last=(final and k == KCH - 1))
                    if final and i < 3:
                        last.then_inc(y_done.sem, 1)
                last.then_inc(w_used.sem, 1)

            def ffn(L, f):
                q0 = f * FFN2_0 // RING
                gu = (GU_BANK, GU_BANK + 1)
                if f == 0:
                    def first_weights():
                        wait(w_lo_half, L, 1)
                        return w_hi[:, 0, :], w_lo[:, 0, :]

                    first_product(L, 0, first_weights, lambda: weights(L, 0, 1), N512, gu, gu_done,
                                  halfway=lambda: weights(L, 0, 0))
                else:
                    first_product(L, 2, lambda: weights(L, q0, 0), lambda: weights(L, q0, 1), N512, gu, gu_done)

                def chunk(j, between=None):
                    w = weights(L, q0 + j - 1, 2)
                    project(w, N512, gu, 0, xT, 2,
                            before=lambda t: wait(act_done, L, (f * NCH + j - 1) * TB + t + 1))
                    turn_hidden(L, f, j - 1)
                    project(weights(L, q0 + j, 0), N512, gu, 1, xT, 2, gu_done)
                    down(L, f, q0 + j, 1, j - 1, between)

                def turn_last(i):
                    if i == 2:
                        turn_hidden(L, f, NCH - 1)

                def turn_next(i):
                    if i == 3:
                        turn_norm(L, 2 * f + 1, 0, 0)

                chunk(1)
                with nc.tensor.Fori(2, NCH - 1) as j:
                    chunk(j)
                chunk(NCH - 1, turn_last)
                down(L, f, q0 + NCH - 1, 2, NCH - 1, turn_next)
                turn_norm(L, 2 * f + 1, 0, 1)

            def free(L, p, part):
                if p:
                    wait(part_lo, L, part_count(p - 1, part))

            def pair_queries(L, p):
                hi, lo = mix_weights(L, M_PAIR + 2 * p)
                for part, tile0 in ((QN, 0), (QRO, 2)):
                    free(L, p, part)
                    for i in range(2):
                        for k in range(3):
                            cols = slice(k * N512 + (tile0 + i) * P, k * N512 + (tile0 + i + 1) * P)
                            last = passes(psum[:, 2 + part, i * S:(i + 1) * S], hi[:, cols], lo[:, cols],
                                          qlT[:, 0, k, :], qlT[:, 1, k, :], first=(k == 0), last=(k == 2))
                    if part == QN:
                        last.then_inc(part_done.sem, 1)
                last.then_inc(w_used.sem, 1)

            def pair_keys(L, p):
                hi, lo = mix_weights(L, M_PAIR + 2 * p + 1)
                free(L, p, KN)
                for i in range(2):
                    for k in range(2):
                        cols = slice(k * N512 + i * 2 * P, k * N512 + i * 2 * P + P)
                        last = passes(psum[:, 2 + KN, i * S:(i + 1) * S], hi[:, cols], lo[:, cols],
                                      kvT[:, 0, k, :], kvT[:, 1, k, :], first=(k == 0), last=(k == 1))
                last.then_inc(part_done.sem, 1)
                free(L, p, VV)

                def values(w, k):
                    return w[:, k * N512:(k + 1) * N512].rearrange("p (h c n) -> p h c n", h=2, c=2)[:, :, 1, :]
                for t in range(TB):
                    for k in range(2):
                        last = passes(psum[:, 2 + VV, t * S:(t + 1) * S].rearrange("p (h n) -> p h n", h=2),
                                      kvT[:, 0, k, blk(t)], kvT[:, 1, k, blk(t)],
                                      values(hi, k), values(lo, k), first=(k == 0), last=(k == 1))
                last.then_inc(w_used.sem, 1)

            def pair_scores(L, p):
                wait(part_lo, L, part_count(p, KN))
                if p:
                    wait(exp_done, L, p)
                else:
                    wait(pool_scaled, L, 2)
                q, qr, k = pair(p, QN), pair(p, QRO), pair(p, KN)
                for t, bank, n in ((1, 6, S), (0, 7, P)):
                    for i in range(2):
                        dst = psum[:, bank, i * n:(i + 1) * n]
                        passes(dst, q[:, 0, i, blk(t)], q[:, 1, i, blk(t)], k[:, 0, i, 0:n], k[:, 1, i, 0:n],
                               first=True, last=False)
                        nc.tensor.matmul(dst[:, n - P:n], ident_r[:, :], causal_r[:, :], start=False, stop=False)
                        last = passes(dst, qr[:, 0, i, blk(t)], qr[:, 1, i, blk(t)], krT[:, 0, 0:n], krT[:, 1, 0:n],
                                      first=False, last=True)
                last.then_inc(score_done.sem, 1)

            def turn_probs(L, p):
                wait(prob_done, L, p + 1)
                if p:
                    wait(o_lo, L, p)
                row = scores[:, p % 2, :]
                for i in range(2):
                    for dst, src in ((psum[:, 0, i * S:i * S + P], 2 * S + i * P),
                                     (psum[:, 0, i * S + P:(i + 1) * S], i * S),
                                     (psum[:, 1, i * P:(i + 1) * P], i * S + P)):
                        last = nc.tensor.transpose(dst, row[:, src:src + P], ident[:, :])
                last.then_inc(prob_tr.sem, 1)

            def pair_values(L, p):
                wait(prob_lo, L, p + 1)
                wait(part_lo, L, part_count(p, VV))
                v = pair(p, VV)
                for i in range(2):
                    c = slice(i * P, (i + 1) * P)
                    passes(psum[:, 0, i * S:(i + 1) * S], v[:, 0, 0, c], v[:, 1, 0, c],
                           small_T[:, 0, i * S:(i + 1) * S], small_T[:, 1, i * S:(i + 1) * S], first=True, last=False)
                    late = slice(2 * S + i * P, 2 * S + (i + 1) * P)
                    last = passes(psum[:, 0, i * S + P:(i + 1) * S], v[:, 0, 1, c], v[:, 1, 1, c],
                                  small_T[:, 0, late], small_T[:, 1, late], first=False, last=True)
                last.then_inc(pv_done.sem, 1)

            def latent(L, i):
                bank, src = ((4, qlat_s), (2, kvlat_s))[i]
                wait(lat_normed, L, i + 1)
                if i:
                    wait(krot_step, L, 4)
                for t in range(TB):
                    tiles(psum[:, bank + t, :], src[:, t, :], 3, lat_tr)

            def window_sums(L):
                wait(xp_lo, L, TB)
                for g in range(PG):
                    dst = psum[:, 6 + g // 2, (g % 2) * S:(g % 2 + 1) * S]
                    c = slice(g * P, (g + 1) * P)
                    early, late = window[:, g * S:(g + 1) * S], window[:, PG * S + g * P:PG * S + (g + 1) * P]
                    for i in range(2):
                        nc.tensor.matmul(dst, xpt[:, i, 0, c], early, start=(i == 0), stop=False)
                    for i in range(2):
                        last = nc.tensor.matmul(dst[:, P:], xpt[:, i, 1, c], late, start=False, stop=(i == 1))
                last.then_inc(pool_done.sem, 1)

            def pool_mix(L):
                hi, lo = mix_weights(L, M_MAPS)
                wait(pool_lo, L, 1)
                for g in range(PG):
                    c = slice(g * P, (g + 1) * P)
                    last = passes(psum[:, 6 + g // 2, (g % 2) * S:(g % 2 + 1) * S], hi[:, c], lo[:, c],
                                  poolT[:, 0, g, :], poolT[:, 1, g, :], first=True, last=True)
                last.then_inc(w_used.sem, 1)

            def gate(L, c, m):
                def free(t):
                    if c:
                        wait(gate_biased, L, TB * (c - 1) + t + 1)

                project(mix_weights(L, m), N512, (0, 1), 0, xT, 2, before=free)
                project(mix_weights(L, m + 1), N512, (0, 1), 1, xT, 2, gate_done)

            def mixer(L):
                first_product(L, 1, lambda: mix_weights(L, M_Q), lambda: mix_weights(L, M_Q + 1), QR, (4, 5), q_done)
                project(mix_weights(L, M_KV), KVW, (2, 3), 0, xT, 2)
                project(mix_weights(L, M_KV + 1), KVW, (2, 3), 1, xT, 2, kv_done)
                project(mix_weights(L, M_POOL), POOL, (6, 7), 0, xT, 2)
                project(mix_weights(L, M_POOL + 1), POOL, (6, 7), 1, xT, 2, xp_done)
                gate(L, 0, M_G0)
                latent(L, 0)
                gate(L, 1, M_G1)
                latent(L, 1)
                wait(rotary_ready, L, 1)
                window_sums(L)
                gate(L, 2, M_G2)
                pool_mix(L)
                gate(L, 3, M_G3)
                wait(lat_lo, L, 2 * TB)
                pair_queries(L, 0)
                pair_keys(L, 0)
                pair_queries(L, 1)
                pair_keys(L, 1)
                pair_scores(L, 0)
                pair_queries(L, 2)
                pair_keys(L, 2)
                wait(gate_biased, L, 4 * TB)
                turn_probs(L, 0)
                pair_scores(L, 1)
                pair_queries(L, 3)
                pair_values(L, 0)
                pair_keys(L, 3)
                turn_probs(L, 1)
                pair_scores(L, 2)
                w = mix_weights(L, M_PP)
                wait(part_lo, L, part_count(3, QRO))
                wait(pool_lo, L, 2)
                project(w, N512, (2, 3), 0, mixT, 1, a_done, before=lambda t: pair_values(L, 1) if t else None)
                turn_probs(L, 2)
                pair_scores(L, 3)
                w = mix_weights(L, M_PP + 1)
                wait(part_lo, L, part_count(3, VV))
                project(w, N512, (4, 5), 0, mixT, 1, a_done, before=lambda t: pair_values(L, 2) if t else None)
                turn_probs(L, 3)
                w = mix_weights(L, M_AP)
                wait(a_gated, L, TB)
                wait(o_lo, L, 2)
                project(w, N512, (2, 3), 0, oT, 2)
                pair_values(L, 3)
                w = mix_weights(L, M_AP + 1)
                wait(a_gated, L, 2 * TB)
                project(w, N512, (4, 5), 0, oT, 2)
                w = mix_weights(L, M_AP + 2)
                wait(o_lo, L, PAIRS)
                project(w, N512, (2, 3), 1, oT, 2, b_done)
                project(mix_weights(L, M_AP + 3), N512, (4, 5), 1, oT, 2, b_done,
                        before=lambda t: turn_merged(L, 0, 0) if t else None)
                turn_merged(L, 0, 1)

                def merged_first(t):
                    if t:
                        turn_merged(L, 1, 0)
                    wait(mrg_lo, L, t + 1)
                w = mix_weights(L, M_WO)
                project(w, N512, (0, 2), 0, xT, 2, before=merged_first)
                turn_merged(L, 1, 1)
                w = mix_weights(L, M_WO + 1)
                project(w, N512, (0, 2), 1, xT, 2, y_done, before=lambda t: wait(mrg_lo, L, TB + t + 1))
                project(mix_weights(L, M_WO + 2), N512, (1, 3), 0, xT, 2)
                project(mix_weights(L, M_WO + 3), N512, (1, 3), 1, xT, 2, y_done,
                        before=lambda t: turn_norm(L, 2, 0, 0) if t else None)
                turn_norm(L, 2, 0, 1)

            pe.sem_inc(w_used.sem, RING)
            pe.wait_ge(ident_landed, 16)
            for t in range(TB):
                turn_norm(0, 0, 0, t)
            with nc.tensor.Fori(0, DEPTH) as L:
                ffn(L, 0)
                mixer(L)
                ffn(L, 1)


_CONSTANTS = ("c_ident", "c_causal", "c_window", "c_inv_count", "c_rotary")
_INS = ("ffn1_up", "ffn1_down", "w_in", "b_gate", "pool_maps", "pool_scale", "w_pool_proj", "q_latent_norm",
        "w_uq", "kv_latent_norm", "w_ukv", "w_attn_proj", "w_out", "ffn2_up", "ffn2_down")


def kernel(**inputs):
    import concourse.bacc as _bacc
    from concourse.bass_utils import run_bass_kernel_spmd as _run

    nc = _bacc.Bacc("TRN2", target_bir_lowering=False, num_devices=1)
    arrays = {name: np.ascontiguousarray(inputs[name]) for name in ("x", "positions") + _INS}
    rows = [inputs[name][layer] for layer in range(DEPTH) for name in ("norm_ffn1", "norm_mix", "norm_ffn2")]
    arrays["gains"] = np.ascontiguousarray(np.stack(rows + [inputs["final_norm"]]))
    arrays.update(shape_constants())
    names = ("x", "positions", "gains") + _INS + _CONSTANTS
    args = [nc.dram_tensor(name + "_dram", arrays[name].shape, mybir.dt.from_np(arrays[name].dtype),
                           kind="ExternalInput").ap() for name in names]
    out = nc.dram_tensor("out_dram", arrays["x"].shape, F32, kind="ExternalOutput").ap()
    trunk(nc, *args, out)
    r = _run(nc, [{name + "_dram": arrays[name] for name in names}], core_ids=[0])
    return r.results[0]["out_dram"]
```
